# Optimizing a Trainium2 kernel written in Bass

```python
import math
import jax, jax.numpy as jnp
from jax import lax
import numpy as np

D_MODEL = 1024
BATCH = 1
SEQ = 128
DEPTH = 2
DEC_BATCH = 1
DEC_SEQ = 128
PAST_LEN = 128

GRID_W = 64
EPS = 1e-6
ROPE_BASE = 10000.0
QBLOCK = 128
H_A = 4
DH_A = 64
DV_A = 2 * DH_A
W_A = H_A * DV_A
C_B = 512
SHORT_K = 3
H_EMB = 33
H_FFN = 64
H_FAST_DECAY = 0.3
H_SLOW_DECAY = 1.5
H_TARGET = 1e-2
H_C = 4
DK_C = 64
DV_C = 128
W_C = H_C * DV_C
CHUNK = 128
N_EXPERTS = 16
N_GROUPS = 4
EXP_PER_GROUP = N_EXPERTS // N_GROUPS
TOP_K = 2
D_FF = 512
SPLIT_SIZES = (H_A * 2 * DH_A, H_A * 2 * DH_A, W_A, 3 * C_B, H_C * DK_C, H_C * DK_C, W_C, W_C)
D_IN = 2 * H_A * 2 * DH_A + W_A + 3 * C_B + 2 * H_C * DK_C + 2 * W_C

kernel_name = 'hybrid_diffattn_hyena_retnet_groupmoe_prefix'

def split_points():
    pts, acc = [], 0
    for s in SPLIT_SIZES[:-1]:
        acc += s
        pts.append(acc)
    return pts

def rms_norm(x, g=None):
    xf = x.astype(jnp.float32)
    y = (xf * lax.rsqrt(jnp.mean(xf * xf, axis=-1, keepdims=True) + EPS)).astype(x.dtype)
    return y if g is None else y * g

def axial_rope(n, dim):
    rows = n // GRID_W
    row = jnp.repeat(jnp.arange(rows, dtype=jnp.float32), GRID_W)
    col = jnp.tile(jnp.arange(GRID_W, dtype=jnp.float32), rows)
    quarter = dim // 4
    inv = ROPE_BASE ** (-jnp.arange(quarter, dtype=jnp.float32) / quarter)
    ar = row[:, None] * inv
    ac = col[:, None] * inv
    ang = jnp.concatenate([ar, ar, ac, ac], axis=-1)
    return jnp.cos(ang), jnp.sin(ang)

def apply_rope(x, cos, sin):
    shape = (1, x.shape[1]) + (1,) * (x.ndim - 3) + (x.shape[-1],)
    c = cos.reshape(shape).astype(x.dtype)
    s = sin.reshape(shape).astype(x.dtype)
    a, b, cc, d = jnp.split(x, 4, axis=-1)
    rot = jnp.concatenate([-b, a, -d, cc], axis=-1)
    return x * c + rot * s

def diff_attention(q, k, v, lam, lam_init, subln_g):
    bsz, lq = q.shape[:2]
    nb = lq // QBLOCK
    qb = q.reshape(bsz, nb, QBLOCK, H_A, 2, DH_A).transpose(1, 0, 2, 3, 4, 5)
    scale = DH_A ** -0.5

    def block(qi):
        s = jnp.einsum('bqhcd,bkhcd->bchqk', qi, k).astype(jnp.float32) * scale
        p = jax.nn.softmax(s, axis=-1)
        a = (p[:, 0] - lam * p[:, 1]).astype(v.dtype)
        return jnp.einsum('bhqk,bkhe->bqhe', a, v)

    o = lax.map(block, qb)
    o = o.transpose(1, 0, 2, 3, 4).reshape(bsz, lq, H_A, DV_A)
    o = rms_norm(o, subln_g) * (1.0 - lam_init)
    return o.reshape(bsz, lq, W_A)

def short_conv(u, w, bias):
    pad = SHORT_K // 2
    L = u.shape[1]
    up = jnp.pad(u, ((0, 0), (pad, pad), (0, 0)))
    out = bias
    for j in range(SHORT_K):
        out = out + up[:, j:j + L] * w[j]
    return out

def hyena_filter(L, f_w1, f_b1, f_w2, f_b2, f_w3):
    f32 = jnp.float32
    t = jnp.linspace(0.0, 1.0, L, dtype=f32)[:, None]
    bands = (H_EMB - 1) // 2
    w = 2.0 * math.pi * jnp.arange(L, dtype=f32)[:, None] / L
    fr = jnp.linspace(1e-4, bands - 1, bands, dtype=f32)
    z = jnp.concatenate([t, jnp.cos(w * fr), -jnp.sin(w * fr)], axis=-1)
    hid = jnp.sin(z @ f_w1.astype(f32) + f_b1.astype(f32))
    hid = jnp.sin(hid @ f_w2.astype(f32) + f_b2.astype(f32))
    h = (hid @ f_w3.astype(f32)).reshape(L, 2, C_B)
    max_decay = math.log(H_TARGET) / H_FAST_DECAY
    min_decay = math.log(H_TARGET) / H_SLOW_DECAY
    deltas = jnp.linspace(min_decay, max_decay, C_B, dtype=f32)
    h = h * jnp.exp(-t * jnp.abs(deltas))[:, None, :]
    h = h / jnp.sum(jnp.abs(h), axis=(0, 1), keepdims=True)
    return jnp.concatenate([h[:, 0], jnp.zeros((1, C_B), f32), jnp.flip(h[1:, 1], axis=0)], axis=0)

def long_conv(u, filt, skip):
    L = u.shape[1]
    uf = jnp.fft.rfft(u.astype(jnp.float32), n=2 * L, axis=1)
    ff = jnp.fft.rfft(filt, n=2 * L, axis=0)
    y = jnp.fft.irfft(uf * ff[None], n=2 * L, axis=1)[:, :L]
    return (y + u.astype(jnp.float32) * skip.astype(jnp.float32)).astype(u.dtype)

def hyena_mixer(u, conv_w, conv_b, f_w1, f_b1, f_w2, f_b2, f_w3, skip):
    L = u.shape[1]
    uc = short_conv(u, conv_w, conv_b)
    x0, x1, v = jnp.split(uc, 3, axis=-1)
    filt = hyena_filter(L, f_w1, f_b1, f_w2, f_b2, f_w3)
    return x0 * long_conv(v * x1, filt, skip)

def retention_scan(q, k, v, log_gamma, s0):
    dt = q.dtype
    f32 = jnp.float32
    bsz, L = q.shape[:2]
    nc = L // CHUNK
    pos = jnp.arange(CHUNK, dtype=f32)
    lg = log_gamma.astype(f32)[:, None]
    diff = pos[:, None] - pos[None, :]
    dmask = jnp.where(diff >= 0, jnp.exp(lg[:, :, None] * jnp.maximum(diff, 0.0)), 0.0)
    xi = jnp.exp(lg * (pos + 1.0)).T[:, :, None]
    zeta = jnp.exp(lg * (CHUNK - 1.0 - pos)).T[:, :, None]
    g_blk = jnp.exp(lg[:, 0] * CHUNK)[:, None, None]

    def chunks(a):
        return a.astype(f32).reshape(bsz, nc, CHUNK, a.shape[2], a.shape[3]).swapaxes(0, 1)

    def step(S, xs):
        qi, ki, vi = xs
        att = jnp.einsum('bnhd,bmhd->bhnm', qi, ki) * dmask
        inner = jnp.einsum('bhnm,bmhe->bnhe', att, vi)
        cross = jnp.einsum('bnhd,bhde->bnhe', qi, S) * xi
        S = g_blk * S + jnp.einsum('bmhd,bmhe->bhde', ki * zeta, vi)
        return S, inner + cross

    S, o = lax.scan(step, s0.astype(f32), (chunks(q), chunks(k), chunks(v)))
    o = o.swapaxes(0, 1).reshape(bsz, L, H_C, DV_C)
    return o.astype(dt), S.astype(dt)

def bidir_retention(q, k, v, lg_f, lg_b, s0_f, s0_b):
    of, sf = retention_scan(q, k, v, lg_f, s0_f)
    ob, sb = retention_scan(jnp.flip(q, 1), jnp.flip(k, 1), jnp.flip(v, 1), lg_b, s0_b)
    return of + jnp.flip(ob, 1), sf, sb

def moe(h, w_router, b_router, w1, w3, w2):
    scores = jax.nn.softmax((h @ w_router).astype(jnp.float32), axis=-1)
    sel = scores + b_router.astype(jnp.float32)
    grp = sel.reshape(sel.shape[:-1] + (N_GROUPS, EXP_PER_GROUP))
    gscore = lax.top_k(grp, TOP_K)[0].sum(-1)
    gidx = jnp.argmax(gscore, axis=-1)
    gmask = gidx[..., None] == jnp.arange(N_GROUPS)
    masked = jnp.where(gmask[..., None], grp, -jnp.inf).reshape(sel.shape)
    _, eidx = lax.top_k(masked, TOP_K)
    wsel = jnp.take_along_axis(scores, eidx, axis=-1)
    wsel = wsel / jnp.sum(wsel, axis=-1, keepdims=True)
    gate = jnp.sum((eidx[..., None] == jnp.arange(N_EXPERTS)).astype(jnp.float32) * wsel[..., None], axis=-2)
    a = jnp.einsum('bld,edf->blef', h, w1)
    b = jnp.einsum('bld,edf->blef', h, w3)
    act = jax.nn.silu(a) * b * gate[..., None].astype(h.dtype)
    return jnp.einsum('blef,efd->bld', act, w2)

def trunk_layer(x, cond, p, layer, w_router, b_router, rope, ctx):
    bsz, L, _ = x.shape
    mod = jax.nn.silu(cond) @ p['w_ada'] + p['b_ada']
    sh1, sc1, g1, sh2, sc2, g2 = jnp.split(mod, 6, axis=-1)
    h = rms_norm(x, p['norm1']) * (1 + sc1) + sh1
    qa, ka, va, hy, qr, kr, vr, gr = jnp.split(h @ p['w_in'], split_points(), axis=-1)
    qa = qa.reshape(bsz, L, H_A, 2, DH_A)
    ka = ka.reshape(bsz, L, H_A, 2, DH_A)
    va = va.reshape(bsz, L, H_A, DV_A)
    qr = qr.reshape(bsz, L, H_C, DK_C)
    kr = kr.reshape(bsz, L, H_C, DK_C) * (DK_C ** -0.5)
    vr = vr.reshape(bsz, L, H_C, DV_C)
    if ctx is None:
        k_all, v_all = ka, va
        s0_f = jnp.zeros((bsz, H_C, DK_C, DV_C), jnp.float32)
        s0_b = s0_f
    else:
        k_ctx, v_ctx, s0_f, s0_b = ctx
        (cos_a, sin_a), (cos_c, sin_c) = rope
        qa = apply_rope(qa, cos_a, sin_a)
        ka = apply_rope(ka, cos_a, sin_a)
        qr = apply_rope(qr, cos_c, sin_c)
        kr = apply_rope(kr, cos_c, sin_c)
        k_c = k_ctx.reshape(bsz, k_ctx.shape[1], H_A, 2, DH_A).astype(ka.dtype)
        k_all = jnp.concatenate([k_c, ka], axis=1)
        v_all = jnp.concatenate([v_ctx.astype(va.dtype), va], axis=1)
    al = p['attn_lambda'].astype(jnp.float32)
    lam_init = 0.8 - 0.6 * math.exp(-0.3 * layer)
    lam = jnp.exp(jnp.sum(al[0] * al[1])) - jnp.exp(jnp.sum(al[2] * al[3])) + lam_init
    ya = diff_attention(qa, k_all, v_all, lam, lam_init, p['attn_subln_g'])
    yb = hyena_mixer(hy, p['hy_conv_w'], p['hy_conv_b'], p['hy_f_w1'], p['hy_f_b1'],
                     p['hy_f_w2'], p['hy_f_b2'], p['hy_f_w3'], p['hy_skip'])
    lg = jnp.log1p(-jnp.exp2(-p['ret_decay_exp'].astype(jnp.float32)))
    o_r, sf, sb = bidir_retention(qr, kr, vr, lg[0], lg[1], s0_f, s0_b)
    yc = rms_norm(o_r).reshape(bsz, L, W_C) * jax.nn.silu(gr)
    ga, gb, gc = jnp.split(jax.nn.sigmoid(h @ p['w_gate'] + p['b_gate']), 3, axis=-1)
    merged = ga * (ya @ p['w_branch_a']) + gb * (yb @ p['w_branch_b']) + gc * (yc @ p['w_branch_c'])
    x = x + g1 * (merged @ p['w_out'])
    h2 = rms_norm(x, p['norm2']) * (1 + sc2) + sh2
    x = x + g2 * moe(h2, w_router, b_router, p['moe_w1'], p['moe_w3'], p['moe_w2'])
    return x, (ka.reshape(bsz, L, H_A, 2 * DH_A), va, sf, sb)

def setup_inputs(seed: int = 0) -> dict:
    key = jax.random.key(seed)
    ks = iter(jax.random.split(key, 48))
    f32 = jnp.float32

    def nrm(shape, scale):
        return jax.random.normal(next(ks), shape, f32) * scale

    def gain(shape):
        return 1.0 + nrm(shape, 0.02)

    return {
        'x_prompt': nrm((BATCH, SEQ, D_MODEL), 1.0),
        'x_sample': nrm((DEC_BATCH, DEC_SEQ, D_MODEL), 1.0),
        'cache_attn_k': nrm((DEC_BATCH, DEPTH, PAST_LEN, H_A, 2 * DH_A), 1.0),
        'cache_attn_v': nrm((DEC_BATCH, DEPTH, PAST_LEN, H_A, DV_A), 1.0),
        'state_retention': nrm((DEC_BATCH, DEPTH, 2, H_C, DK_C, DV_C), 1.0),
        'c': nrm((DEC_BATCH, D_MODEL), 1.0),
        'c_ctx': nrm((D_MODEL,), 1.0),
        'w_ada': nrm((DEPTH, D_MODEL, 6 * D_MODEL), 0.5 * D_MODEL ** -0.5),
        'b_ada': nrm((DEPTH, 6 * D_MODEL), 0.02),
        'norm1_g': gain((DEPTH, D_MODEL)),
        'norm2_g': gain((DEPTH, D_MODEL)),
        'final_g': gain((D_MODEL,)),
        'w_in': nrm((DEPTH, D_MODEL, D_IN), D_MODEL ** -0.5),
        'attn_lambda': nrm((DEPTH, 4, DH_A), 0.1),
        'attn_subln_g': gain((DEPTH, DV_A)),
        'hy_conv_w': nrm((DEPTH, SHORT_K, 3 * C_B), SHORT_K ** -0.5),
        'hy_conv_b': nrm((DEPTH, 3 * C_B), 0.02),
        'hy_f_w1': nrm((DEPTH, H_EMB, H_FFN), H_EMB ** -0.5),
        'hy_f_b1': nrm((DEPTH, H_FFN), 0.02),
        'hy_f_w2': nrm((DEPTH, H_FFN, H_FFN), H_FFN ** -0.5),
        'hy_f_b2': nrm((DEPTH, H_FFN), 0.02),
        'hy_f_w3': nrm((DEPTH, H_FFN, 2 * C_B), H_FFN ** -0.5),
        'hy_skip': nrm((DEPTH, C_B), 0.1),
        'ret_decay_exp': 5.0 + jnp.arange(H_C, dtype=f32) + jax.random.uniform(next(ks), (DEPTH, 2, H_C), f32, 0.0, 0.5),
        'w_branch_a': nrm((DEPTH, W_A, D_MODEL), W_A ** -0.5),
        'w_branch_b': nrm((DEPTH, C_B, D_MODEL), C_B ** -0.5),
        'w_branch_c': nrm((DEPTH, W_C, D_MODEL), W_C ** -0.5),
        'w_gate': nrm((DEPTH, D_MODEL, 3 * D_MODEL), D_MODEL ** -0.5),
        'b_gate': nrm((DEPTH, 3 * D_MODEL), 0.02),
        'w_out': nrm((DEPTH, D_MODEL, D_MODEL), D_MODEL ** -0.5),
        'w_router': nrm((D_MODEL, N_EXPERTS), D_MODEL ** -0.5),
        'b_router': nrm((N_EXPERTS,), 0.01),
        'moe_w1': nrm((DEPTH, N_EXPERTS, D_MODEL, D_FF), D_MODEL ** -0.5),
        'moe_w3': nrm((DEPTH, N_EXPERTS, D_MODEL, D_FF), D_MODEL ** -0.5),
        'moe_w2': nrm((DEPTH, N_EXPERTS, D_FF, D_MODEL), D_FF ** -0.5),
    }

def reference(x_prompt, x_sample, cache_attn_k, cache_attn_v, state_retention, c, c_ctx,
              w_ada, b_ada, norm1_g, norm2_g, final_g, w_in, attn_lambda, attn_subln_g,
              hy_conv_w, hy_conv_b, hy_f_w1, hy_f_b1, hy_f_w2, hy_f_b2, hy_f_w3, hy_skip,
              ret_decay_exp, w_branch_a, w_branch_b, w_branch_c, w_gate, b_gate, w_out,
              w_router, b_router, moe_w1, moe_w3, moe_w2):
    def layer_params(l):
        return {
            'w_ada': w_ada[l], 'b_ada': b_ada[l], 'norm1': norm1_g[l], 'norm2': norm2_g[l],
            'w_in': w_in[l], 'attn_lambda': attn_lambda[l], 'attn_subln_g': attn_subln_g[l],
            'hy_conv_w': hy_conv_w[l], 'hy_conv_b': hy_conv_b[l], 'hy_f_w1': hy_f_w1[l],
            'hy_f_b1': hy_f_b1[l], 'hy_f_w2': hy_f_w2[l], 'hy_f_b2': hy_f_b2[l],
            'hy_f_w3': hy_f_w3[l], 'hy_skip': hy_skip[l], 'ret_decay_exp': ret_decay_exp[l],
            'w_branch_a': w_branch_a[l], 'w_branch_b': w_branch_b[l], 'w_branch_c': w_branch_c[l],
            'w_gate': w_gate[l], 'b_gate': b_gate[l], 'w_out': w_out[l],
            'moe_w1': moe_w1[l], 'moe_w3': moe_w3[l], 'moe_w2': moe_w2[l],
        }

    x = x_prompt
    ks, vs, ss = [], [], []
    for l in range(DEPTH):
        x, (k_l, v_l, sf, sb) = trunk_layer(x, c_ctx, layer_params(l), l, w_router, b_router, None, None)
        ks.append(k_l)
        vs.append(v_l)
        ss.append(jnp.stack([sf, sb], axis=1))
    y_prompt = rms_norm(x, final_g)
    new_attn_k = jnp.stack(ks, axis=1)
    new_attn_v = jnp.stack(vs, axis=1)
    new_retention_state = jnp.stack(ss, axis=1)

    n = x_sample.shape[1]
    rope = (axial_rope(n, DH_A), axial_rope(n, DK_C))
    cond = c[:, None, :]
    x = x_sample
    for l in range(DEPTH):
        ctx = (cache_attn_k[:, l], cache_attn_v[:, l], state_retention[:, l, 0], state_retention[:, l, 1])
        x, _ = trunk_layer(x, cond, layer_params(l), l, w_router, b_router, rope, ctx)
    y_sample = rms_norm(x, final_g)
    return (y_prompt, y_sample, new_attn_k, new_attn_v, new_retention_state)


_drawn_inputs = setup_inputs


def setup_inputs(seed=0):
    import zlib

    import numpy as np

    out = dict(_drawn_inputs(seed))
    spreads = {}
    factors = {'final_g': 7.911,
     'attn_subln_g': 3.573,
     'hy_conv_b': 8.0,
     'hy_f_b1': 8.0,
     'hy_f_b2': 11.596,
     'b_gate': 3.63}
    for name, (base, spread) in spreads.items():
        noise = np.random.default_rng([zlib.crc32(name.encode()), seed]).standard_normal(out[name].shape)
        drawn = base * np.exp(spread * noise) if base else spread * noise
        out[name] = __import__('jax').numpy.asarray(drawn.astype(out[name].dtype))
    for name, factor in factors.items():
        out[name] = (out[name] * factor).astype(out[name].dtype)
    return out
```

```python
import math
from contextlib import ExitStack

import numpy as np
import concourse.bass as bass
from concourse import mybir

F32 = mybir.dt.float32
ALU = mybir.AluOpType
ACT = mybir.ActivationFunctionType
AX = mybir.AxisListType

P = 128
D = 1024
DEPTH = 2
SEQ = 128
GROUPS = 2
TOK = GROUPS * SEQ
KT = D // P
EPS = 1e-6
GRID_W = 64
ROPE_BASE = 10000.0
H_A, DH_A, DV_A = 4, 64, 128
C_B = 512
SHORT_K = 3
H_EMB, H_FFN = 33, 64
H_C, DK_C, DV_C = 4, 64, 128
N_EXPERTS, N_GROUPS, EPG = 16, 4, 4
D_FF = 512
BIG = 1.0e30
TWO_PI_HI = 6.28125
TWO_PI_LO = 2.0 * math.pi - 6.28125
ROUND = 12582912.0
SIN_EDGE = 3.1415925

PIECE = 2048
SLOTS = 8
W_IN_ORDER = [1536 + 256 * i for i in range(6)] + [3072, 3328, 3584, 3840, 0, 256, 512, 768,
                                                   1024, 1280, 4096, 4352]
U_HY, U_QR, U_KR, U_VR, U_QA, U_KA, U_VA, U_GR, U_GATE, U_MERGE, U_OUT = (
    0, 6, 7, 8, 10, 12, 14, 16, 18, 30, 42)
N_PROJ = 46
ADA_PIECES = 24


def lam_init(layer):
    return 0.8 - 0.6 * math.exp(-0.3 * layer)


def columns(*parts):
    at, out = 0, {}
    for name, n in parts:
        out[name] = (at, at + n)
        at += n
    return out, at


PAR, N_PAR = columns(("b_ada", 48), ("norm1", 8), ("norm2", 8), ("conv_w", 36), ("conv_b", 12),
                     ("skip", 4), ("b_gate", 24), ("subln", 1), ("lam", 256), ("rde", 8),
                     ("rde_q", 4), ("f_w1", 64), ("f_b1", 1), ("f_w2", 64), ("f_b2", 1),
                     ("f_w3", 1024))
CST, N_CST = columns(("ident", 128), ("rot", 128), ("cos", 128), ("sin", 128), ("cf", 128),
                     ("sf", 128), ("s0", 128), ("nq", 128), ("cf1", 128), ("s1", 128),
                     ("nq1", 128), ("ic", 128), ("is", 128), ("z", 128), ("decay", 512),
                     ("xf", 128), ("xb", 128), ("df", 128), ("db", 128), ("mf", 128),
                     ("mb", 128), ("zf", 1), ("zb", 1))
SHD, N_SHD = columns(("final", 8), ("router", 128), ("b_router", 16), ("cond", 16))


def constant_columns():
    c = np.zeros((P, N_CST), np.float64)

    def put(name, a):
        a = np.asarray(a)
        c[:a.shape[0], CST[name][0]:CST[name][1]] = a

    i = np.arange(P)
    put("ident", np.eye(P))
    rot = np.zeros((P, P))
    q = DH_A // 4
    for b in range(0, P, 2 * q):
        for j in range(q):
            rot[b + q + j, b + j] = -1.0
            rot[b + j, b + q + j] = 1.0
    put("rot", rot)
    inv = (np.float32(ROPE_BASE) ** (-np.arange(q, dtype=np.float32) / np.float32(q)))
    row, col = (i // GRID_W).astype(np.float32), (i % GRID_W).astype(np.float32)
    ar, ac = row[:, None] * inv, col[:, None] * inv
    ang = np.concatenate([ar, ar, ac, ac], -1)
    put("cos", np.tile(np.cos(ang), (1, 2)).T)
    put("sin", np.tile(np.sin(ang), (1, 2)).T)
    w = 2 * np.pi * np.outer(i, i) / (2 * SEQ)
    alt = (-1.0) ** i
    cf, sf, s0, nq = np.cos(w), -np.sin(w), -np.sin(w), np.cos(w)
    sf[:, 0] = alt
    s0[:, 0] = 0.0
    nq[:, 0] = alt
    cf1, nq1 = cf.copy(), nq.copy()
    cf1[0] = nq1[0] = 0.0
    for name, a in (("cf", cf), ("sf", sf), ("s0", s0), ("nq", nq), ("cf1", cf1), ("s1", -s0),
                    ("nq1", nq1)):
        put(name, a)
    ic, isn = 2 * np.cos(w) / (2 * SEQ), -2 * np.sin(w) / (2 * SEQ)
    ic[0] = 1.0 / (2 * SEQ)
    isn[0] = alt / (2 * SEQ)
    put("ic", ic)
    put("is", isn)
    t = np.linspace(0.0, 1.0, SEQ, dtype=np.float32)[:, None]
    bands = (H_EMB - 1) // 2
    wt = (np.float32(2.0 * math.pi) * np.arange(SEQ, dtype=np.float32)[:, None] / np.float32(SEQ))
    fr = np.linspace(1e-4, bands - 1, bands, dtype=np.float32)
    a = wt * fr
    put("z", np.concatenate([t, np.cos(a), -np.sin(a)], -1).T)
    deltas = np.linspace(math.log(1e-2) / 1.5, math.log(1e-2) / 0.3, C_B, dtype=np.float32)
    put("decay", np.exp(-t * np.abs(deltas)))
    one = np.ones((P, 1))
    put("xf", one * (i + 1)[None])
    put("xb", one * (SEQ - i)[None])
    d = i[None, :] - i[:, None]
    put("df", np.maximum(d, 0))
    put("db", np.maximum(-d, 0))
    put("mf", d >= 0)
    put("mb", d <= 0)
    put("zf", (SEQ - 1 - i)[:, None])
    put("zb", i[:, None])
    return c.astype(np.float32)


def trunk_program(nc, weights, params, consts, shared, x_in, k_cache, v_cache, s_cache,
                  y_out, k_out, v_out, s_out):
    with ExitStack() as ctx:
        def sem(name):
            return ctx.enter_context(nc.semaphore(name))

        s_act_ready = sem("act_ready")
        s_amixT_ready = sem("amixT_ready")
        s_amix_ready = sem("amix_ready")
        s_att_out = sem("att_out")
        s_att_scores = sem("att_scores")
        s_att_turned = sem("att_turned")
        s_attr_ready = sem("attr_ready")
        s_b_half = sem("b_half")
        s_bank_free = [sem(f"bank_free{b}") for b in range(8)]
        s_cache_in = sem("cache_in")
        s_cond_ready = sem("cond_ready")
        s_cond_tanh = sem("cond_tanh")
        s_consts_in = sem("consts_in")
        s_conv_mid = sem("conv_mid")
        s_decay_exp = sem("decay_exp")
        s_decay_ln = sem("decay_ln")
        s_decay_log = sem("decay_log")
        s_decay_one = sem("decay_one")
        s_dft_done = sem("dft_done")
        s_expert_done = sem("expert_done")
        s_ff_sum = sem("ff_sum")
        s_ff_tanh = sem("ff_tanh")
        s_gate_ready = sem("gate_ready")
        s_gate_wide = sem("gate_wide")
        s_gates_turned = sem("gates_turned")
        s_gr_tanh = sem("gr_tanh")
        s_gt_ready = sem("gt_ready")
        s_h_ready_s = sem("h_ready_s")
        s_h_ready_v = sem("h_ready_v")
        s_h_scaled = sem("h_scaled")
        s_hid = [sem(f"hid{n}") for n in range(3)]
        s_hid_arg = sem("hid_arg")
        s_hid_sum = sem("hid_sum")
        s_idft_done = sem("idft_done")
        s_ktok_sum = sem("ktok_sum")
        s_kz_ready = sem("kz_ready")
        s_lam_exp = sem("lam_exp")
        s_lam_sums = sem("lam_sums")
        s_logits = sem("logits")
        s_logits_exp = sem("logits_exp")
        s_logits_shifted = sem("logits_shifted")
        s_max_ready = sem("max_ready")
        s_merged = sem("merged")
        s_mod_ready = sem("mod_ready")
        s_mod_sum = sem("mod_sum")
        s_norm_mean = sem("norm_mean")
        s_norm_root = sem("norm_root")
        s_norm_sum = sem("norm_sum")
        s_o_mean = sem("o_mean")
        s_o_norm_sum = sem("o_norm_sum")
        s_o_root = sem("o_root")
        s_o_sum = sem("o_sum")
        s_ones_set = sem("ones_set")
        s_osq_ready = sem("osq_ready")
        s_params_in = sem("params_in")
        s_params_used = sem("params_used")
        s_proj_done = sem("proj_done")
        s_qa_copied = sem("qa_copied")
        s_qa_roped = sem("qa_roped")
        s_qkr_copied = sem("qkr_copied")
        s_qkr_roped = sem("qkr_roped")
        s_qx_ready = sem("qx_ready")
        s_ret_scores = sem("ret_scores")
        s_rotated = sem("rotated")
        s_scalar_link = sem("scalar_link")
        s_shared_in = sem("shared_in")
        s_spectrum_sum = sem("spectrum_sum")
        s_state_copied = sem("state_copied")
        s_state_sum = sem("state_sum")
        s_stored = sem("stored")
        s_stores_read = sem("stores_read")
        s_tables_exp = sem("tables_exp")
        s_taps = sem("taps")
        s_taps_abs = sem("taps_abs")
        s_taps_decayed = sem("taps_decayed")
        s_taps_norm = sem("taps_norm")
        s_taps_sum = sem("taps_sum")
        s_va_copied = sem("va_copied")
        s_vector_link = sem("vector_link")
        s_vr_copied = sem("vr_copied")
        s_weights_in = [sem(f"weights_in{slot}") for slot in range(SLOTS)]
        s_weights_used = sem("weights_used")
        s_x_in = sem("x_in")
        s_x_mixed = sem("x_mixed")
        s_x_moe = sem("x_moe")
        s_x_squared = sem("x_squared")
        s_y_ready = sem("y_ready")
        s_ya_ready = sem("ya_ready")
        s_yb_ready = sem("yb_ready")
        s_yc_ready = sem("yc_ready")
        s_ysp_ready = sem("ysp_ready")
        s_z_ready = sem("z_ready")
        s_zeros_set = sem("zeros_set")
        s_zt_ready = sem("zt_ready")
        s_zt_sum = sem("zt_sum")

        def sb(name, *shape):
            return ctx.enter_context(nc.sbuf_tensor(name, list(shape), F32))

        ring = sb("ring", P, SLOTS, PIECE)
        cst = sb("cst", P, N_CST)
        shd = sb("shd", P, N_SHD)
        par = sb("par", P, N_PAR)
        x = sb("x", P, KT, TOK)
        h = sb("h", P, KT, TOK)
        gates = sb("gates", P, 24, TOK)
        uc = sb("uc", P, 12, TOK)
        qk = sb("qk", P, 8, TOK)
        qkr = sb("qkr", P, 4, TOK)
        va = sb("va", P, GROUPS, 512)
        vr = sb("vr", P, GROUPS, 512)
        gr = sb("gr", P, 4, TOK)
        kc = sb("kc", P, H_A, SEQ)
        vc = sb("vc", P, H_A * DV_A)
        sc = sb("sc", P, H_C, 2, DV_C)
        filt = sb("filt", P, 3, C_B)
        zt = sb("zt", P, C_B)
        ysp = sb("ysp", P, 2, C_B)
        tmp = sb("tmp", P, C_B)
        attr = sb("attr", P, H_C, SEQ)
        qx = sb("qx", P, 2, 2, SEQ)
        dsum = sb("dsum", P, H_C, SEQ)
        xi = sb("xi", P, 2, 2, SEQ)
        probs = sb("probs", P, 2, 2, 2 * SEQ)
        amix = sb("amix", P, 2, 2 * SEQ)
        amixT = sb("amixT", P, 2, 2 * SEQ)
        osq = zt
        rinv = sb("rinv", P, C_B)
        rms = sb("rms", P, TOK)
        rmsi = sb("rmsi", P, TOK)
        ones = sb("ones", P, P)
        zeros = sb("zeros", P, P)
        modT = sb("modT", P, 48, 2)
        amp = sb("amp", P, 2, 8, 2)
        condT = sb("condT", P, 8, 2)
        sm = sb("sm", P, 640)
        kz = probs[:, 0, :, :]
        sout = qkr[0:64, :, :].rearrange("p a b -> p (a b)").rearrange("p (a b) -> p a b", a=2)
        gt = sb("gt", N_EXPERTS, TOK)
        rt = sb("rt", P, 12, 2, N_EXPERTS)
        pair = sb("pair", P, 8, 6)

        lgs, lgu, lgm, zeta, lamv, b_half, subg, neglam = (
            sm[:, 0:12], sm[:, 16:28], sm[:, 32:44], sm[:, 48:56], sm[:, 64:68], sm[:, 72:96],
            sm[:, 100:101], sm[:, 104:105])
        lgd, lgn = sm[:, 112:124], sm[:, 128:140]
        mx, sums, rsum = sm[:, 144:148], sm[:, 152:156], sm[:, 160:164]
        hid = sm[:, 176:304]
        rnd = sm[:, 304:432]
        arg = sm[:, 432:560]
        red = sm[:, 560:592]
        hs = uc[:, 0:4, :].rearrange("p a b -> p (a b)").rearrange("p (a b) -> p a b", a=2)
        habs = uc[:, 4:8, :].rearrange("p a b -> p (a b)").rearrange("p (a b) -> p a b", a=2)
        merged = uc[:, 4:12, :]
        th = gates[:, 0:2, :]
        sact = gates[:, 2:4, :]
        act = gates[:, 4:12, :]

        bank = [ctx.enter_context(nc.psum_tensor(f"bank{b}", [P, 512], F32)) for b in range(8)]

        def C(name, rows=P):
            return cst[0:rows, CST[name][0]:CST[name][1]]

        def R(name, rows=P):
            return par[0:rows, PAR[name][0]:PAR[name][1]]

        def H(name):
            return shd[:, SHD[name][0]:SHD[name][1]]

        ident = C("ident")

        def heads(b, n=4):
            return bank[b][:, 0:n * 128].rearrange("p (a b) -> p a b", a=n)

        def tiles(b):
            return bank[b][:, :].rearrange("p (a b) -> p a b", a=2)

        def g_cols(g):
            return slice(g * SEQ, (g + 1) * SEQ)

        block = ctx.enter_context(nc.Block())

        @block.sync
        def _(sp):
            def load(slot, n):
                sp.dma_start(ring[:, slot, :], weights[n, :, :]).then_inc(s_weights_in[slot], 16)

            for slot in range(SLOTS):
                load(slot, slot)
            laps = weights.rearrange("(l s) p c -> l s p c", s=SLOTS)
            with sp.Fori(1, laps.shape[0]) as lap:
                for slot in range(SLOTS):
                    sp.wait_ge(s_weights_used, lap * SLOTS + (slot + 1 - SLOTS))
                    sp.dma_start(ring[:, slot, :], laps[bass.ds(lap, 1), slot, :, :].rearrange(
                        "a p c -> (a p) c")).then_inc(s_weights_in[slot], 16)

        @block.gpsimd
        def _(pool):
            pool.dma_start(cst[:, :], consts).then_inc(s_consts_in, 16)
            pool.dma_start(shd[:, :], shared).then_inc(s_shared_in, 16)
            pool.memset(ones[:, :], 1.0).then_inc(s_ones_set, 1)
            pool.memset(zeros[:, :], 0.0).then_inc(s_zeros_set, 1)
            for layer in range(DEPTH):
                if layer:
                    pool.wait_ge(s_params_used, layer - 1 + 1)
                pool.dma_start(par[:, :], params[layer, :, :]).then_inc(s_params_in, 16)
                if layer == 0:
                    pool.dma_start(x[:, :, :], x_in).then_inc(s_x_in, 16)
                pool.dma_start(kc[:, :, :], k_cache[layer]).then_inc(s_cache_in, 16)
                pool.dma_start(vc[:, :], v_cache[layer]).then_inc(s_cache_in, 16)
                pool.dma_start(sc[:, :, :, :], s_cache[layer]).then_inc(s_cache_in, 16)
                pool.wait_ge(s_qa_copied, 4 * layer + 4)
                pool.dma_start(k_out[layer], qk[:, 4:8, 0:SEQ]).then_inc(s_stored, 16)
                pool.wait_ge(s_va_copied, 2 * layer + 2)
                pool.dma_start(v_out[layer], va[:, 0, :]).then_inc(s_stored, 16)
                pool.wait_ge(s_state_copied, 2 * layer + 2)
                for way in range(2):
                    pool.dma_start(s_out[layer, way], sout[:, way, :]).then_inc(s_stored, 16)
                pool.wait_ge(s_stored, 16 * 4 * (layer + 1))
                pool.sem_inc(s_stores_read, 1)
            pool.wait_ge(s_y_ready, 1)
            pool.dma_start(y_out, h[:, :, :]).then_inc(s_stored, 16)
            pool.wait_ge(s_stored, 16 * (4 * DEPTH + 1))

        @block.tensor
        def _(pe):
            held = [0] * 8
            pieces = [0]

            def take(b):
                if held[b]:
                    pe.wait_ge(s_bank_free[b], held[b])
                held[b] += 1

            def piece(width):
                n = pieces[0]
                pieces[0] += 1
                pe.wait_ge(s_weights_in[n % SLOTS], 16 * (n // SLOTS + 1))
                return ring[:, n % SLOTS, :].rearrange("p (k n) -> p k n", n=width)

            def then(bank_, event):
                pe.matmul(bank_[0:32, 510:512], zeros[:, 0:32], zeros[:, 0:2], start=False, stop=False,
                          skip_group_check=True).then_inc(event, 1)

            def ada(layer, j):
                w = piece(256)
                if j == 0:
                    take(7)
                for c in range(2):
                    col = 2 * (2 * j + c)
                    for k in range(KT):
                        last = pe.matmul(bank[7][:, col:col + 2], w[:, k, c * P:(c + 1) * P],
                                         condT[:, k, :], start=(k == 0), stop=(k == KT - 1))
                last.then_inc(s_weights_used, 1)
                if j == ADA_PIECES - 1:
                    pe.matmul(bank[7][:, 510:512], zeros[:, :], condT[:, 0, :], start=True,
                              stop=True).then_inc(s_mod_sum, 1)

            def filter_step(layer, n):
                if n == 0:
                    pe.wait_ge(s_consts_in, 16)
                    pe.wait_ge(s_params_in, 16 * (layer + 1))
                    take(4)
                    pe.matmul(bank[4][0:64, 0:128], R("f_w1", H_EMB), C("z", H_EMB), start=True,
                              stop=True).then_inc(s_hid_sum, 1)
                elif n == 1:
                    pe.wait_ge(s_hid[1], layer + 1)
                    take(4)
                    pe.matmul(bank[4][0:64, 0:128], R("f_w2", 64), hid[0:64, :], start=True,
                              stop=True).then_inc(s_hid_sum, 1)
                elif n == 2:
                    pe.wait_ge(s_hid[2], layer + 1)
                    for c in range(2):
                        take(4 + c)
                        w3 = R("f_w3", 64)[:, c * 512:(c + 1) * 512]
                        pe.matmul(bank[4 + c][:, :], hid[0:64, :], w3, start=True,
                                  stop=True).then_inc(s_taps_sum, 1)
                elif n == 3:
                    pe.wait_ge(s_taps_abs, layer + 1)
                    take(6)
                    for c in range(2):
                        last = pe.matmul(bank[6][:, :], ones[:, :], habs[:, c, :], start=(c == 0),
                                         stop=(c == 1))
                    last.then_inc(s_taps_norm, 1)
                else:
                    pe.wait_ge(s_taps, layer + 1)
                    for b, a0, a1 in ((4, "cf", "cf1"), (5, "s0", "s1"), (6, "nq", "nq1")):
                        take(b)
                        pe.matmul(bank[b][:, :], C(a0), hs[:, 0, :], start=True, stop=False)
                        pe.matmul(bank[b][:, :], C(a1), hs[:, 1, :], start=False,
                                  stop=True).then_inc(s_spectrum_sum, 1)

            def norm_sum(count):
                take(4)
                for k in range(KT):
                    if k % 4 == 0:
                        pe.wait_ge(s_x_squared, 2 * count + k // 4 + 1)
                    last = pe.matmul(bank[4][:, 0:TOK], ones[:, :], h[:, k, :], start=(k == 0),
                                     stop=(k == KT - 1))
                last.then_inc(s_norm_sum, 1)

            def proj(layer, u):
                b = u % 4
                w = piece(256)
                take(b)
                norms = 2 * layer
                if U_VR <= u < U_QA or U_VA <= u < U_GR:
                    for g in range(GROUPS):
                        for k in range(KT):
                            last = pe.matmul(bank[b][:, g * 256:(g + 1) * 256], h[:, k, g_cols(g)],
                                             w[:, k, :], start=(k == 0), stop=(k == KT - 1))
                else:
                    for c in range(2):
                        for k in range(KT):
                            if u == 0 and c == 0:
                                pe.wait_ge(s_h_ready_v, KT * norms + k + 1)
                                pe.wait_ge(s_h_ready_s, KT * norms + k + 1)
                            last = pe.matmul(bank[b][:, c * TOK:(c + 1) * TOK],
                                             w[:, k, c * P:(c + 1) * P], h[:, k, :],
                                             start=(k == 0), stop=(k == KT - 1))
                last.then_inc(s_weights_used, 1)
                then(bank[b], s_proj_done)

            def z_transpose(layer, g):
                pe.wait_ge(s_z_ready, layer + 1)
                take(4)
                for c in range(4):
                    last = pe.transpose(bank[4][:, c * P:(c + 1) * P], uc[:, 8 + c, g_cols(g)], ident)
                last.then_inc(s_zt_sum, 1)

            def rope(layer, n, src, b):
                if n == 0:
                    pe.wait_ge(s_qkr_copied, 2 * layer + 2)
                else:
                    pe.wait_ge(s_qa_copied, 4 * layer + 2 * n)
                take(b)
                pe.matmul(bank[b][:, :], C("rot"), src, start=True, stop=True).then_inc(s_rotated, 1)

            def dft(layer, g):
                pe.wait_ge(s_zt_ready, 2 * layer + g + 1)
                for b, t in ((6, "cf"), (7, "sf")):
                    take(b)
                    pe.matmul(bank[b][:, :], C(t), zt[:, :], start=True, stop=True).then_inc(
                        s_dft_done, 1)

            def idft(layer, g):
                pe.wait_ge(s_ysp_ready, 2 * layer + g + 1)
                take(5)
                for c in range(4):
                    pe.matmul(bank[5][:, c * P:(c + 1) * P], ysp[:, 0, c * P:(c + 1) * P], C("ic"),
                              start=True, stop=False)
                    last = pe.matmul(bank[5][:, c * P:(c + 1) * P], ysp[:, 1, c * P:(c + 1) * P],
                                     C("is"), start=False, stop=True)
                last.then_inc(s_idft_done, 1)

            def ret_scores(layer, g):
                pe.wait_ge(s_qkr_copied, 2 * layer + 2)
                if g:
                    pe.wait_ge(s_qkr_roped, layer + 1)
                for b in (4, 5):
                    take(b)
                for hh in range(H_C):
                    r = slice(64 * (hh % 2), 64 * (hh % 2) + 64)
                    last = pe.matmul(bank[4 + hh % 2][:, (hh // 2) * P:(hh // 2 + 1) * P],
                                     qkr[r, 2 + hh // 2, g_cols(g)], qkr[r, hh // 2, g_cols(g)],
                                     start=True, stop=True)
                last.then_inc(s_ret_scores, 1)

            def ret_out(layer, g):
                pe.wait_ge(s_attr_ready, 2 * layer + g + 1)
                pe.wait_ge(s_vr_copied, 2 * layer + 2)
                take(6)
                for hh in range(H_C):
                    o = bank[6][:, hh * P:(hh + 1) * P]
                    last = pe.matmul(o, vr[:, g, hh * P:(hh + 1) * P], attr[:, hh, :], start=True,
                                     stop=(g == 0))
                    if g:
                        pe.wait_ge(s_qx_ready, layer + 1)
                        pe.wait_ge(s_cache_in, 48 * (layer + 1))
                        for way in range(2):
                            last = pe.matmul(o, sc[:, hh, way, :], qx[:, hh // 2, way, :],
                                             start=False, stop=(way == 1))
                last.then_inc(s_o_sum, 1)

            def k_transpose(layer):
                take(4)
                for t in range(2):
                    last = pe.transpose(bank[4][:, t * P:(t + 1) * P], qkr[:, 2 + t, 0:SEQ], ident)
                last.then_inc(s_ktok_sum, 1)

            def states(layer):
                pe.wait_ge(s_kz_ready, layer + 1)
                for way in range(2):
                    take(4 + way)
                    for hh in range(H_C):
                        last = pe.matmul(bank[4 + way][0:64, hh * P:(hh + 1) * P],
                                         kz[:, way, hh * 64:(hh + 1) * 64],
                                         vr[:, 0, hh * P:(hh + 1) * P], start=True, stop=True)
                    last.then_inc(s_state_sum, 1)

            def o_norm(layer, j):
                pe.wait_ge(s_osq_ready, 4 * layer + j + 1)
                take(7)
                pe.matmul(bank[7][:, :], ones[:, :], osq[:, :], start=True, stop=True).then_inc(
                    s_o_norm_sum, 1)

            def att_scores(layer, i):
                g, hh = i // 4, i % 4
                pe.wait_ge(s_qa_copied, 4 * layer + 4)
                if g:
                    pe.wait_ge(s_qa_roped, 2 * layer + 2)
                    pe.wait_ge(s_cache_in, 48 * (layer + 1))
                for c in range(2):
                    r = slice(64 * c, 64 * c + 64)
                    take(4 + c)
                    q = qk[r, hh, g_cols(g)]
                    if g:
                        pe.matmul(bank[4 + c][:, 0:SEQ], q, kc[r, hh, :], start=True, stop=True)
                    last = pe.matmul(bank[4 + c][:, g * SEQ:(g + 1) * SEQ], q,
                                     qk[r, 4 + hh, g_cols(g)], start=True, stop=True)
                    last.then_inc(s_att_scores, 1)

            def att_turn(layer, i):
                g = i // 4
                pe.wait_ge(s_amix_ready, 8 * layer + i + 1)
                take(7)
                for t in range(g + 1):
                    last = pe.transpose(bank[7][:, t * P:(t + 1) * P],
                                        amix[:, i % 2, t * P:(t + 1) * P], ident)
                last.then_inc(s_att_turned, 1)

            def att_out(layer, i):
                g, hh = i // 4, i % 4
                pe.wait_ge(s_amixT_ready, 8 * layer + i + 1)
                pe.wait_ge(s_va_copied, 2 * layer + 2)
                if hh == 0:
                    take(6)
                cols = slice(hh * P, (hh + 1) * P)
                if g:
                    pe.matmul(bank[6][:, cols], vc[:, cols], amixT[:, i % 2, 0:P], start=True,
                              stop=False)
                last = pe.matmul(bank[6][:, cols], va[:, g, cols], amixT[:, i % 2, g * P:(g + 1) * P],
                                 start=(g == 0), stop=True)
                last.then_inc(s_att_out, 1)
                if hh == 3:
                    then(bank[6], s_o_sum)

            def merge(layer):
                u = U_MERGE
                for half in range(2):
                    for branch, src, event in ((1, uc, s_yb_ready), (2, gr, s_yc_ready),
                                               (0, qk, s_ya_ready)):
                        w = piece(512)
                        pe.wait_ge(event, 2 * layer + 2)
                        for dp in range(2):
                            b = u % 4
                            take(b)
                            for c in range(2):
                                d = 2 * dp + c
                                for k in range(4):
                                    last = pe.matmul(bank[b][:, c * TOK:(c + 1) * TOK],
                                                     w[:, k, d * P:(d + 1) * P], src[:, k, :],
                                                     start=(k == 0), stop=(k == 3))
                            if dp == 0:
                                last.then_inc(s_proj_done, 1)
                            u += 1
                        last.then_inc(s_weights_used, 1)
                        then(bank[b], s_proj_done)

            def out_proj(layer):
                for u in range(U_OUT, N_PROJ):
                    b = u % 4
                    w = piece(256)
                    take(b)
                    for c in range(2):
                        for k in range(KT):
                            if c == 0 and u == U_OUT and k % 2 == 0:
                                pe.wait_ge(s_merged, 4 * layer + k // 2 + 1)
                            last = pe.matmul(bank[b][:, c * TOK:(c + 1) * TOK],
                                             w[:, k, c * P:(c + 1) * P], merged[:, k, :],
                                             start=(k == 0), stop=(k == KT - 1))
                    last.then_inc(s_weights_used, 1)
                    then(bank[b], s_proj_done)

            def route(layer):
                take(5)
                for g in range(GROUPS):
                    for k in range(KT):
                        if g == 0:
                            pe.wait_ge(s_h_ready_v, KT * (2 * layer + 1) + k + 1)
                            pe.wait_ge(s_h_ready_s, KT * (2 * layer + 1) + k + 1)
                        last = pe.matmul(bank[5][:, g * 16:(g + 1) * 16], h[:, k, g_cols(g)],
                                         H("router")[:, k * 16:(k + 1) * 16], start=(k == 0),
                                         stop=(k == KT - 1))
                last.then_inc(s_logits, 1)

            def gates_turn(layer):
                pe.wait_ge(s_gate_ready, layer + 1)
                take(5)
                for g in range(GROUPS):
                    last = pe.transpose(bank[5][0:16, g_cols(g)], rt[:, 11, g, :], ident)
                last.then_inc(s_gates_turned, 1)

            def moe_in(layer, e):
                if e == 0:
                    pe.wait_ge(s_gt_ready, layer + 1)
                take(7)
                pe.matmul(bank[7][:, 0:TOK], ident[0:N_EXPERTS, e:e + 1].broadcast_to([N_EXPERTS, P]), gt[:, :], start=True, stop=True).then_inc(
                    s_gate_wide, 1)
                for half in range(2):
                    w1, w3 = piece(256), piece(256)
                    for c in range(2):
                        n = 4 * e + 2 * half + c
                        b = 4 + n % 3
                        take(b)
                        for j, w in enumerate((w1, w3)):
                            for k in range(KT):
                                last = pe.matmul(bank[b][:, j * TOK:(j + 1) * TOK],
                                                 w[:, k, c * P:(c + 1) * P], h[:, k, :],
                                                 start=(k == 0), stop=(k == KT - 1))
                        if c == 0:
                            last.then_inc(s_ff_sum, 1)
                    last.then_inc(s_weights_used, 2)
                    then(bank[b], s_ff_sum)

            def moe_out(layer, e):
                for half in range(2):
                    w = piece(512)
                    for d in range(4):
                        dt = 4 * half + d
                        for f in range(4):
                            if half == 0 and d == 0:
                                pe.wait_ge(s_act_ready, 64 * layer + 4 * e + f + 1)
                            last = pe.matmul(bank[dt // 2][:, (dt % 2) * TOK:(dt % 2 + 1) * TOK],
                                             w[:, f, d * P:(d + 1) * P],
                                             act[:, 4 * (e % 2) + f, :], start=False, stop=False,
                                             skip_group_check=True)
                    last.then_inc(s_weights_used, 1)
                then(bank[0], s_expert_done)

            pe.wait_ge(s_cond_ready, 1)
            pe.wait_ge(s_ones_set, 1)
            pe.wait_ge(s_zeros_set, 1)
            for layer in range(DEPTH):
                for j in range(ADA_PIECES):
                    ada(layer, j)
                    if j in (2, 5, 8, 12, 16):
                        filter_step(layer, (2, 5, 8, 12, 16).index(j))
                    if j == 20:
                        norm_sum(2 * layer)
                for u in range(U_MERGE):
                    proj(layer, u)
                    if u == 7:
                        z_transpose(layer, 0)
                    if u == 8:
                        rope(layer, 0, qkr[:, :, SEQ:TOK], 5)
                    if u == 9:
                        dft(layer, 0)
                    if u == 10:
                        z_transpose(layer, 1)
                    if u == 11:
                        ret_scores(layer, 0)
                    if u == 12:
                        dft(layer, 1)
                    if u == 13:
                        idft(layer, 0)
                        rope(layer, 1, qk[:, 0:4, SEQ:TOK], 4)
                    if u == 14:
                        rope(layer, 2, qk[:, 4:8, SEQ:TOK], 4)
                        ret_out(layer, 0)
                    if u == 15:
                        idft(layer, 1)
                        o_norm(layer, 0)
                    if u == 16:
                        ret_scores(layer, 1)
                    if u == 17:
                        k_transpose(layer)
                        ret_out(layer, 1)
                    if u == 18:
                        o_norm(layer, 1)
                        states(layer)
                    if 19 <= u < 29:
                        i = u - 19
                        if i < 8:
                            att_scores(layer, i)
                        if 1 <= i < 9:
                            att_turn(layer, i - 1)
                        if i >= 2:
                            att_out(layer, i - 2)
                            if i - 2 == 3:
                                o_norm(layer, 2)
                    if u == 29:
                        o_norm(layer, 3)
                merge(layer)
                out_proj(layer)
                norm_sum(2 * layer + 1)
                route(layer)
                gates_turn(layer)
                for b in range(4):
                    take(b)
                    pe.matmul(bank[b][:, :], zeros[:, :], h[:, 0:2, :], start=True, stop=False,
                              skip_group_check=True)
                for e in range(N_EXPERTS):
                    moe_in(layer, e)
                    if e:
                        moe_out(layer, e - 1)
                moe_out(layer, N_EXPERTS - 1)
            norm_sum(2 * DEPTH)

        @block.scalar
        def _(act_e):
            sc_e = act_e
            links = [0]

            def link(ins):
                links[0] += 1
                ins.then_inc(s_scalar_link, 1)
                sc_e.wait_ge(s_scalar_link, links[0])

            def squares(count, source, per):
                for half in range(2):
                    if source is s_x_in:
                        sc_e.wait_ge(s_x_in, 16)
                    else:
                        sc_e.wait_ge(source, per + 2 * half + 2)
                    sc_e.activation(h[:, 4 * half:4 * half + 4, :], x[:, 4 * half:4 * half + 4, :],
                                    ACT.Square).then_inc(s_x_squared, 1)

            def norm(count, which):
                sc_e.wait_ge(s_norm_mean, count + 1)
                sc_e.activation(rms[:, :], rmsi[:, :], ACT.Sqrt).then_inc(s_norm_root, 1)
                if which is None:
                    return
                for k in range(KT):
                    sc_e.wait_ge(s_h_scaled, KT * count + k + 1)
                    sc_e.activation(h[:, k, 0:SEQ], h[:, k, 0:SEQ], ACT.Identity,
                                    scale=amp[:, which, k, 0:1],
                                    bias=modT[:, 24 * which + k, 0:1]).then_inc(s_h_ready_s, 1)

            def o_rms(layer, j):
                sc_e.wait_ge(s_o_sum, 4 * layer + j + 1)
                if 4 * layer + j > 0:
                    sc_e.wait_ge(s_o_norm_sum, 4 * layer + j)
                sc_e.activation(osq[:, :], bank[6][:, :], ACT.Square).then_inc(s_osq_ready, 1)
                sc_e.wait_ge(s_o_mean, 4 * layer + j + 1)
                sc_e.activation(tmp[:, :], rinv[:, :], ACT.Sqrt).then_inc(s_o_root, 1)

            sc_e.wait_ge(s_shared_in, 16)
            cond = H("cond").rearrange("p (a b) -> p a b", a=8)
            sc_e.activation(condT[:, :, :], cond, ACT.Tanh, scale=0.5).then_inc(s_cond_tanh, 1)
            for layer in range(DEPTH):
                sc_e.wait_ge(s_consts_in, 16)
                sc_e.wait_ge(s_params_in, 16 * (layer + 1))
                sc_e.activation(lgs[:, :], par[:, PAR["rde"][0]:PAR["rde_q"][1]], ACT.Exp,
                                scale=-math.log(2.0)).then_inc(s_decay_exp, 1)
                sc_e.wait_ge(s_lam_sums, layer + 1)
                sc_e.activation(lamv[:, 2:4], lamv[:, 0:2], ACT.Exp).then_inc(s_lam_exp, 1)
                sc_e.wait_ge(s_decay_one, layer + 1)
                sc_e.activation(lgn[:, :], lgu[:, :], ACT.Ln).then_inc(s_decay_ln, 1)
                sc_e.wait_ge(s_decay_log, layer + 1)
                for t in range(2):
                    for way, name in enumerate(("xf", "xb")):
                        sc_e.activation(xi[:, t, way, :], C(name), ACT.Exp,
                                        scale=lgm[:, 8 + 2 * t + way:9 + 2 * t + way])
                for hh in range(H_C):
                    sc_e.activation(dsum[:, hh, :], C("df"), ACT.Exp, scale=lgm[:, hh:hh + 1])
                    sc_e.activation(attr[:, hh, :], C("db"), ACT.Exp, scale=lgm[:, 4 + hh:5 + hh])
                sc_e.activation(zeta[:, :], zeta[:, :], ACT.Exp).then_inc(s_tables_exp, 1)
                for n in range(2):
                    sc_e.wait_ge(s_hid_arg, 2 * layer + n + 1)
                    sc_e.activation(hid[0:64, :], arg[0:64, :], ACT.Sin).then_inc(s_hid[n + 1], 1)
                sc_e.wait_ge(s_taps_decayed, layer + 1)
                sc_e.activation(habs[:, :, :], hs[:, :, :], ACT.Abs).then_inc(s_taps_abs, 1)
                for n in range(3):
                    sc_e.wait_ge(s_spectrum_sum, 3 * layer + n + 1)
                    sc_e.activation(filt[:, n, :], bank[4 + n][:, :], ACT.Copy).then_inc(
                        s_bank_free[4 + n], 1)
                if layer == 0:
                    squares(0, s_x_in, 0)
                else:
                    squares(2 * layer, s_x_moe, 4 * (layer - 1))
                sc_e.wait_ge(s_mod_ready, layer + 1)
                norm(2 * layer, 0)

                def unit(u):
                    sc_e.wait_ge(s_proj_done, N_PROJ * layer + u + 1)
                    return bank[u % 4], tiles(u % 4), s_bank_free[u % 4]

                for u in range(U_HY, U_HY + 6):
                    _, src, _ = unit(u)
                    for c in range(2):
                        t = 2 * u + c
                        sc_e.activation(uc[:, t, :], src[:, c, :], ACT.Identity,
                                        scale=R("conv_w")[:, 12 + t:13 + t],
                                        bias=R("conv_b")[:, t:t + 1]).then_inc(s_conv_mid, 1)

                def copy_out(u):
                    full, src, free = unit(u)
                    if u in (U_QR, U_KR):
                        if layer and u == U_QR:
                            sc_e.wait_ge(s_stores_read, layer)
                        sc_e.activation(qkr[:, 2 * (u - U_QR):2 * (u - U_QR) + 2, :], src, ACT.Copy,
                                        scale=1.0 if u == U_QR else DK_C ** -0.5).then_inc(free, 1)
                        event = s_qkr_copied
                    elif u < U_QA:
                        sc_e.activation(vr[:, :, 256 * (u - U_VR):256 * (u - U_VR) + 256], src,
                                        ACT.Copy).then_inc(free, 1)
                        event = s_vr_copied
                    elif u < U_VA:
                        t = 2 * (u - U_QA)
                        sc_e.activation(qk[:, t:t + 2, :], src, ACT.Copy).then_inc(free, 1)
                        event = s_qa_copied
                    else:
                        sc_e.activation(va[:, :, 256 * (u - U_VA):256 * (u - U_VA) + 256], src,
                                        ACT.Copy).then_inc(free, 1)
                        event = s_va_copied
                    sc_e.wait_ge(free, copies_of(layer, u))
                    sc_e.sem_inc(event, 1)

                def copies_of(layer, u):
                    per = [len([v for v in range(N_PROJ) if v % 4 == b]) + 1 for b in range(4)]
                    return layer * per[u % 4] + u // 4 + 1

                def zt_copy(g):
                    sc_e.wait_ge(s_zt_sum, 2 * layer + g + 1)
                    if 2 * (2 * layer + g) > 0:
                        sc_e.wait_ge(s_dft_done, 2 * (2 * layer + g))
                    sc_e.activation(zt[:, :], bank[4][:, :], ACT.Copy).then_inc(s_zt_ready, 1)
                    sc_e.wait_ge(s_zt_ready, 2 * layer + g + 1)
                    sc_e.sem_inc(s_bank_free[4], 1)

                def gate(u):
                    _, src, free = unit(u)
                    if u == U_GATE:
                        sc_e.wait_ge(s_b_half, layer + 1)
                    for c in range(2):
                        t = 2 * (u - U_GATE) + c
                        last = sc_e.activation(gates[:, t, :], src[:, c, :], ACT.Tanh, scale=0.5,
                                               bias=b_half[:, t:t + 1])
                    last.then_inc(free, 1)

                def softmax(i):
                    g = i // 4
                    n = 128 * (g + 1)
                    sc_e.wait_ge(s_max_ready, 8 * layer + i + 1)
                    if 8 * layer + i - 1 > 0:
                        sc_e.wait_ge(s_amix_ready, 8 * layer + i - 1)
                    for c in range(2):
                        sc_e.activation(probs[:, i % 2, c, 0:n], bank[4 + c][:, 0:n], ACT.Exp,
                                        scale=DH_A ** -0.5, bias=mx[:, 2 + c:3 + c],
                                        accum_out=sums[:, c:c + 1]).then_inc(s_bank_free[4 + c], 1)

                def turn_copy(i):
                    g = i // 4
                    n = 128 * (g + 1)
                    sc_e.wait_ge(s_att_turned, 8 * layer + i + 1)
                    if 8 * layer + i - 1 > 0:
                        sc_e.wait_ge(s_att_out, 8 * layer + i - 1)
                    sc_e.activation(amixT[:, i % 2, 0:n], bank[7][:, 0:n], ACT.Copy).then_inc(
                        s_amixT_ready, 1)
                    sc_e.wait_ge(s_amixT_ready, 8 * layer + i + 1)
                    sc_e.sem_inc(s_bank_free[7], 1)

                def state_copy():
                    for way in range(2):
                        sc_e.wait_ge(s_state_sum, 2 * layer + way + 1)
                        sc_e.activation(sout[:, way, :], bank[4 + way][0:64, :], ACT.Copy).then_inc(
                            s_state_copied, 1)
                        sc_e.wait_ge(s_state_copied, 2 * layer + way + 1)
                        sc_e.sem_inc(s_bank_free[4 + way], 1)

                copy_out(6)
                copy_out(7)
                zt_copy(0)
                for u in (8, 9, 10):
                    copy_out(u)
                zt_copy(1)
                for u in (11, 12, 13, 14):
                    copy_out(u)
                o_rms(layer, 0)
                copy_out(15)
                for u in (16, 17):
                    _, src, _ = unit(u)
                    t = 2 * (u - U_GR)
                    sc_e.activation(gr[:, t:t + 2, :], src, ACT.Tanh, scale=0.5).then_inc(
                        s_gr_tanh, 1)
                o_rms(layer, 1)
                gate(18)
                state_copy()
                for u in range(19, 30):
                    gate(u)
                    i = u - 19
                    if i < 8:
                        softmax(i)
                    if 1 <= i < 9:
                        turn_copy(i - 1)
                    if i - 2 == 3:
                        o_rms(layer, 2)
                    if i - 2 == 7:
                        o_rms(layer, 3)
                squares(2 * layer + 1, s_x_mixed, 4 * layer)
                norm(2 * layer + 1, 1)
                sc_e.wait_ge(s_logits_shifted, layer + 1)
                sc_e.activation(rt[:, 0, :, :], rt[:, 0, :, :], ACT.Exp).then_inc(s_logits_exp, 1)
                for n in range(4 * N_EXPERTS):
                    sc_e.wait_ge(s_ff_sum, 64 * layer + n + 1)
                    if 64 * layer + n - 1 > 0:
                        sc_e.wait_ge(s_act_ready, 64 * layer + n - 1)
                    sc_e.activation(th[:, n % 2, :], bank[4 + n % 3][:, 0:TOK], ACT.Tanh,
                                    scale=0.5).then_inc(s_ff_tanh, 1)
            squares(2 * DEPTH, s_x_moe, 4 * (DEPTH - 1))
            norm(2 * DEPTH, None)

        @block.vector
        def _(dve):
            links = [0]

            def link(ins):
                links[0] += 1
                ins.then_inc(s_vector_link, 1)
                dve.wait_ge(s_vector_link, links[0])

            def tt(out, a, b, op):
                return dve.tensor_tensor(out, a, b, op)

            def ts(out, a, s1, op0, s2=None, op1=None):
                if op1 is None:
                    return dve.tensor_scalar(out, a, s1, None, op0)
                return dve.tensor_scalar(out, a, s1, s2, op0, op1)

            def stt(out, a, s, b, op0, op1):
                return dve.scalar_tensor_tensor(out, a, s, b, op0, op1)

            def norm(count, which):
                dve.wait_ge(s_norm_sum, count + 1)
                link(ts(rmsi[:, :], bank[4][:, 0:TOK], 1.0 / D, ALU.mult, EPS, ALU.add))
                dve.sem_inc(s_bank_free[4], 1)
                dve.sem_inc(s_norm_mean, 1)
                dve.wait_ge(s_norm_root, count + 1)
                link(dve.reciprocal(rmsi[:, :], rms[:, :]))
                for k in range(KT):
                    tt(h[:, k, :], x[:, k, :], rmsi[:, :], ALU.mult).then_inc(s_h_scaled, 1)
                    dve.wait_ge(s_h_scaled, KT * count + k + 1)
                    if which is None:
                        link(ts(h[:, k, :], h[:, k, :], H("final")[:, k:k + 1], ALU.mult))
                    else:
                        ts(h[:, k, SEQ:TOK], h[:, k, SEQ:TOK], amp[:, which, k, 1:2], ALU.mult,
                           modT[:, 24 * which + k, 1:2], ALU.add).then_inc(s_h_ready_v, 1)

            def sine_arg(layer, n):
                dve.wait_ge(s_hid_sum, 2 * layer + n + 1)
                a, r = arg[0:64, :], rnd[0:64, :]
                link(ts(a, bank[4][0:64, 0:128], R(f"f_b{n + 1}", 64), ALU.add))
                dve.sem_inc(s_bank_free[4], 1)
                link(ts(r, a, 1.0 / (2 * math.pi), ALU.mult, ROUND, ALU.add))
                link(ts(r, r, -ROUND, ALU.add))
                link(stt(a, r, -TWO_PI_HI, a, ALU.mult, ALU.add))
                link(stt(a, r, -TWO_PI_LO, a, ALU.mult, ALU.add))
                ts(a, a, SIN_EDGE, ALU.min, -SIN_EDGE, ALU.max).then_inc(s_hid_arg, 1)

            dve.wait_ge(s_shared_in, 16)
            cond = H("cond").rearrange("p (a b) -> p a b", a=8)
            dve.wait_ge(s_cond_tanh, 1)
            link(stt(condT[:, :, :], condT[:, :, :], 1.0, cond, ALU.add, ALU.mult))
            ts(condT[:, :, :], condT[:, :, :], 0.5, ALU.mult).then_inc(s_cond_ready, 1)

            for layer in range(DEPTH):
                dve.wait_ge(s_consts_in, 16)
                dve.wait_ge(s_params_in, 16 * (layer + 1))
                lam = R("lam").rearrange("p (a b c) -> p a b c", a=2, b=2)
                link(tt(probs[:, 0, :, 0:64], lam[:, :, 0, :], lam[:, :, 1, :], ALU.mult))
                dve.tensor_reduce(lamv[:, 0:2], probs[:, 0, :, 0:64], AX.X, ALU.add).then_inc(
                    s_lam_sums, 1)
                dve.wait_ge(s_lam_exp, layer + 1)
                link(tt(neglam, lamv[:, 3:4], lamv[:, 2:3], ALU.subtract))
                link(ts(neglam, neglam, -lam_init(layer), ALU.add))
                link(ts(subg, R("subln"), 1.0 - lam_init(layer), ALU.mult))
                ts(b_half[:, :], R("b_gate"), 0.5, ALU.mult).then_inc(s_b_half, 1)
                dve.wait_ge(s_decay_exp, layer + 1)
                ts(lgu[:, :], lgs[:, :], -1.0, ALU.mult, 1.0, ALU.add).then_inc(s_decay_one, 1)
                dve.wait_ge(s_decay_ln, layer + 1)
                link(ts(lgd[:, :], lgu[:, :], 1.0, ALU.is_equal))
                link(stt(lgu[:, :], lgu[:, :], -1.0, lgd[:, :], ALU.add, ALU.add))
                link(dve.reciprocal(lgm[:, :], lgu[:, :]))
                link(tt(lgm[:, :], lgm[:, :], lgn[:, :], ALU.mult))
                link(tt(lgm[:, :], lgm[:, :], lgd[:, :], ALU.add))
                link(stt(lgm[:, :], lgs[:, :], -1.0, lgm[:, :], ALU.mult, ALU.mult))
                link(ts(zeta[:, 0:4], lgm[:, 0:4], C("zf"), ALU.mult))
                link(ts(zeta[:, 4:8], lgm[:, 4:8], C("zb"), ALU.mult))
                dve.sem_inc(s_decay_log, 1)
                dve.wait_ge(s_tables_exp, layer + 1)

                def wide(a, n):
                    return a.unsqueeze(1).broadcast_to([P, n, a.shape[-1]])

                link(tt(dsum[:, :, :], dsum[:, :, :], wide(C("mf"), 4), ALU.mult))
                link(tt(attr[:, :, :], attr[:, :, :], wide(C("mb"), 4), ALU.mult))
                link(tt(dsum[:, :, :], dsum[:, :, :], attr[:, :, :], ALU.add))
                sine_arg(layer, 0)
                sine_arg(layer, 1)
                for c in range(2):
                    dve.wait_ge(s_taps_sum, 2 * layer + c + 1)
                    link(tt(hs[:, c, :], bank[4 + c][:, :], C("decay"), ALU.mult))
                    dve.sem_inc(s_bank_free[4 + c], 1)
                dve.sem_inc(s_taps_decayed, 1)
                dve.wait_ge(s_taps_norm, layer + 1)
                link(dve.reciprocal(tmp[:, :], bank[6][:, :]))
                dve.sem_inc(s_bank_free[6], 1)
                link(tt(hs[:, :, :], hs[:, :, :], wide(tmp[:, :], 2), ALU.mult))
                dve.sem_inc(s_taps, 1)
                dve.wait_ge(s_mod_sum, layer + 1)
                link(tt(modT[:, :, :], bank[7][:, 0:96].rearrange("p (a b) -> p a b", b=2),
                        R("b_ada").unsqueeze(2).broadcast_to([P, 48, 2]), ALU.add))
                dve.sem_inc(s_bank_free[7], 1)
                for n in range(2):
                    link(stt(amp[:, n, :, :], modT[:, 24 * n + 8:24 * n + 16, :], 1.0,
                             R(f"norm{n + 1}").unsqueeze(2).broadcast_to([P, 8, 2]), ALU.add, ALU.mult))
                link(ts(modT[:, 16:24, :], modT[:, 16:24, :], 0.5, ALU.mult))
                dve.sem_inc(s_mod_ready, 1)
                norm(2 * layer, 0)

                def unit(u):
                    dve.wait_ge(s_proj_done, N_PROJ * layer + u + 1)
                    return tiles(u % 4), s_bank_free[u % 4]

                for u in range(U_HY, U_HY + 6):
                    src, free = unit(u)
                    for c in range(2):
                        t = 2 * u + c
                        dve.wait_ge(s_conv_mid, 12 * layer + 2 * u + 2)
                        s = src[:, c, :].rearrange("p (g t) -> p g t", g=2)
                        o = uc[:, t, :].rearrange("p (g t) -> p g t", g=2)
                        link(stt(o[:, :, 1:SEQ], s[:, :, 0:SEQ - 1], R("conv_w")[:, t:t + 1],
                                 o[:, :, 1:SEQ], ALU.mult, ALU.add))
                        link(stt(o[:, :, 0:SEQ - 1], s[:, :, 1:SEQ],
                                 R("conv_w")[:, 24 + t:25 + t], o[:, :, 0:SEQ - 1], ALU.mult, ALU.add))
                    dve.sem_inc(free, 1)
                link(tt(uc[:, 8:12, :], uc[:, 8:12, :], uc[:, 4:8, :], ALU.mult))
                dve.sem_inc(s_z_ready, 1)

                cosw, sinw = wide(C("cos"), 4), wide(C("sin"), 4)

                def rope(n, dst, b, event):
                    dve.wait_ge(s_rotated, 3 * layer + n + 1)
                    tw = tmp[:, :].rearrange("p (a b) -> p a b", a=4)
                    link(tt(tw, heads(b), sinw, ALU.mult))
                    dve.sem_inc(s_bank_free[b], 1)
                    link(tt(dst, dst, cosw, ALU.mult))
                    link(tt(dst, dst, tw, ALU.add))
                    dve.sem_inc(event, 1)

                def spectrum(g):
                    dve.wait_ge(s_dft_done, 4 * layer + 2 * g + 2)
                    if 2 * layer + g > 0:
                        dve.wait_ge(s_idft_done, 2 * layer + g)
                    ur, ui = bank[6][:, :], bank[7][:, :]
                    link(tt(ysp[:, 0, :], ur, filt[:, 0, :], ALU.mult))
                    link(tt(tmp[:, :], ui, filt[:, 1, :], ALU.mult))
                    link(tt(ysp[:, 0, :], ysp[:, 0, :], tmp[:, :], ALU.subtract))
                    link(tt(ysp[:, 1, :], ur, filt[:, 1, :], ALU.mult))
                    dve.sem_inc(s_bank_free[6], 1)
                    link(tt(tmp[:, :], ui, filt[:, 2, :], ALU.mult))
                    dve.sem_inc(s_bank_free[7], 1)
                    link(tt(ysp[:, 1, :], ysp[:, 1, :], tmp[:, :], ALU.add))
                    dve.sem_inc(s_ysp_ready, 1)

                def hyena_out(g):
                    dve.wait_ge(s_idft_done, 2 * layer + g + 1)
                    tw = tmp[:, :].rearrange("p (a b) -> p a b", a=4)
                    for c in range(4):
                        link(stt(tw[:, c, :], uc[:, 8 + c, g_cols(g)], R("skip")[:, c:c + 1],
                                 bank[5][:, c * P:(c + 1) * P], ALU.mult, ALU.add))
                    dve.sem_inc(s_bank_free[5], 1)
                    link(tt(uc[:, 0:4, g_cols(g)], uc[:, 0:4, g_cols(g)], tw, ALU.mult))
                    dve.sem_inc(s_yb_ready, 1)

                def ret_decay(g):
                    dve.wait_ge(s_ret_scores, 2 * layer + g + 1)
                    if 4 * layer + g > 0:
                        dve.wait_ge(s_o_sum, 4 * layer + g)
                    for odd in range(2):
                        link(tt(attr[:, odd::2, :], heads(4 + odd, 2), dsum[:, odd::2, :], ALU.mult))
                        dve.sem_inc(s_bank_free[4 + odd], 1)
                    dve.sem_inc(s_attr_ready, 1)

                def o_scale(j, b=6):
                    dve.wait_ge(s_o_norm_sum, 4 * layer + j + 1)
                    link(ts(rinv[:, :], bank[7][:, :], 1.0 / DV_A, ALU.mult, EPS, ALU.add))
                    dve.sem_inc(s_bank_free[7], 1)
                    dve.sem_inc(s_o_mean, 1)
                    dve.wait_ge(s_o_root, 4 * layer + j + 1)
                    link(dve.reciprocal(rinv[:, :], tmp[:, :]))

                rw = rinv[:, :].rearrange("p (a b) -> p a b", a=4)

                def yc(g):
                    o_scale(g)
                    link(tt(rw, heads(6), rw, ALU.mult))
                    dve.sem_inc(s_bank_free[6], 1)

                def yc_gate(g):
                    link(stt(gr[:, :, g_cols(g)], rw, 0.5, gr[:, :, g_cols(g)], ALU.mult, ALU.mult))
                    dve.sem_inc(s_yc_ready, 1)

                def ya(g):
                    o_scale(2 + g)
                    link(stt(qk[:, 0:4, g_cols(g)], heads(6), subg, rw, ALU.mult, ALU.mult))
                    dve.sem_inc(s_bank_free[6], 1)
                    dve.sem_inc(s_ya_ready, 1)

                def soft_max(i):
                    g = i // 4
                    n = 128 * (g + 1)
                    for c in range(2):
                        dve.wait_ge(s_att_scores, 16 * layer + 2 * i + c + 1)
                        link(dve.tensor_reduce(mx[:, c:c + 1], bank[4 + c][:, 0:n], AX.X, ALU.max))
                    link(ts(mx[:, 2:4], mx[:, 0:2], -(DH_A ** -0.5), ALU.mult))
                    dve.sem_inc(s_max_ready, 1)

                def soft_mix(i):
                    g = i // 4
                    n = 128 * (g + 1)
                    for c in range(2):
                        dve.wait_ge(s_bank_free[4 + c], att_frees(layer, i, c))
                    if 8 * layer + i - 1 > 0:
                        dve.wait_ge(s_att_turned, 8 * layer + i - 1)
                    link(dve.reciprocal(rsum[:, 0:2], sums[:, 0:2]))
                    link(ts(rsum[:, 1:2], rsum[:, 1:2], neglam, ALU.mult))
                    link(ts(amix[:, i % 2, 0:n], probs[:, i % 2, 0, 0:n], rsum[:, 0:1], ALU.mult))
                    stt(amix[:, i % 2, 0:n], probs[:, i % 2, 1, 0:n], rsum[:, 1:2],
                        amix[:, i % 2, 0:n], ALU.mult, ALU.add).then_inc(s_amix_ready, 1)

                def att_frees(layer, i, c):
                    per, before = ((17 + 4, 12) if c == 0 else (14, 6))
                    return FREES[c][0] * layer + FREES[c][1] + i + 1

                experts4 = len([n for n in range(64) if n % 3 == 0])
                experts5 = len([n for n in range(64) if n % 3 == 1])
                FREES = ((3 + 1 + 1 + 2 + 1 + 2 + 1 + 1 + 1 + 8 + 1 + experts4,
                          3 + 1 + 1 + 2 + 1 + 2 + 1 + 1 + 1),
                         (2 + 1 + 1 + 2 + 1 + 1 + 8 + 2 + experts5,
                          2 + 1 + 1 + 2 + 1 + 1))

                rope(0, qkr[:, :, SEQ:TOK], 5, s_qkr_roped)
                for way in range(2):
                    link(tt(qx[:, :, way, :], qkr[:, 0:2, SEQ:TOK], xi[:, :, way, :], ALU.mult))
                dve.sem_inc(s_qx_ready, 1)
                spectrum(0)
                ret_decay(0)
                spectrum(1)
                hyena_out(0)
                rope(1, qk[:, 0:4, SEQ:TOK], 4, s_qa_roped)
                rope(2, qk[:, 4:8, SEQ:TOK], 4, s_qa_roped)
                hyena_out(1)
                yc(0)
                for u in (16, 17):
                    src, free = unit(u)
                    t = 2 * (u - U_GR)
                    dve.wait_ge(s_gr_tanh, 2 * layer + u - 16 + 1)
                    link(stt(gr[:, t:t + 2, :], gr[:, t:t + 2, :], 1.0, src, ALU.add, ALU.mult))
                    dve.sem_inc(free, 1)
                    if u == 16:
                        ret_decay(1)
                yc_gate(0)
                dve.wait_ge(s_ktok_sum, layer + 1)
                for way in range(2):
                    link(tt(kz[:, way, :].rearrange("p (a b) -> p a b", a=4),
                            bank[4][:, 0:256].rearrange("p (a b) -> p a b", a=4),
                            zeta[:, 4 * way:4 * way + 4].unsqueeze(2).broadcast_to([P, 4, 64]),
                            ALU.mult))
                dve.sem_inc(s_bank_free[4], 1)
                dve.sem_inc(s_kz_ready, 1)
                yc(1)
                yc_gate(1)
                for i in range(10):
                    if i < 8:
                        soft_max(i)
                        soft_mix(i)
                    if i - 2 == 3:
                        ya(0)
                ya(1)
                u = U_MERGE
                for half in range(2):
                    for n, branch in enumerate((1, 2, 0)):
                        for dp in range(2):
                            src, free = unit(u)
                            t = 4 * half + 2 * dp
                            gt_ = gates[:, 8 * branch + t:8 * branch + t + 2, :]
                            m = merged[:, t:t + 2, :]
                            tw = tmp[:, :].rearrange("p (a b) -> p a b", a=2)
                            if n == 0:
                                link(stt(m, gt_, 1.0, src, ALU.add, ALU.mult))
                                dve.sem_inc(free, 1)
                            else:
                                link(stt(tw, gt_, 1.0, src, ALU.add, ALU.mult))
                                dve.sem_inc(free, 1)
                                link(tt(m, m, tw, ALU.add))
                            if n == 2:
                                dve.sem_inc(s_merged, 1)
                            u += 1
                for u in range(U_OUT, N_PROJ):
                    src, free = unit(u)
                    for c in range(2):
                        t = 2 * (u - U_OUT) + c
                        for g in range(GROUPS):
                            link(stt(x[:, t, g_cols(g)], src[:, c, g_cols(g)],
                                     modT[:, 16 + t, g:g + 1], x[:, t, g_cols(g)], ALU.mult, ALU.add))
                    dve.sem_inc(free, 1)
                    dve.sem_inc(s_x_mixed, 1)
                dve.sem_inc(s_params_used, 1)
                norm(2 * layer + 1, 1)
                dve.wait_ge(s_logits, layer + 1)
                lg3 = bank[5][:, 0:32].rearrange("p (a b) -> p a b", a=2)

                def per_token(a):
                    return a.unsqueeze(2).broadcast_to([P, 2, N_EXPERTS])

                e_, sel_, tmp_, oh1, oh2 = (rt[:, n, :, :] for n in range(5))
                link(dve.tensor_reduce(red[:, 0:2], lg3, AX.X, ALU.max))
                link(tt(e_, lg3, per_token(red[:, 0:2]), ALU.subtract))
                dve.sem_inc(s_bank_free[5], 1)
                dve.sem_inc(s_logits_shifted, 1)
                dve.wait_ge(s_logits_exp, layer + 1)
                link(dve.tensor_reduce(red[:, 2:4], e_, AX.X, ALU.add))
                link(dve.reciprocal(red[:, 4:6], red[:, 2:4]))
                link(tt(e_, e_, per_token(red[:, 4:6]), ALU.mult))
                link(tt(sel_, e_, H("b_router").unsqueeze(1).broadcast_to([P, 2, 16]), ALU.add))
                s4 = sel_.rearrange("p a (g e) -> p (a g) e", e=EPG)
                link(tt(pair[:, :, 0:3], s4[:, :, 0:3], s4[:, :, 1:4], ALU.add))
                link(tt(pair[:, :, 3:5], s4[:, :, 0:2], s4[:, :, 2:4], ALU.add))
                link(tt(pair[:, :, 5:6], s4[:, :, 0:1], s4[:, :, 3:4], ALU.add))
                link(dve.tensor_reduce(red[:, 8:16], pair[:, :, :], AX.X, ALU.max))
                gs = red[:, 8:16].rearrange("p (a g) -> p a g", a=2)

                def first_max(out, src, n, order):
                    w = order.unsqueeze(1).broadcast_to([P, 2, n])
                    link(dve.tensor_reduce(red[:, 24:26], src, AX.X, ALU.max))
                    link(tt(out, src, red[:, 24:26].unsqueeze(2).broadcast_to([P, 2, n]),
                            ALU.is_equal))
                    link(tt(out, out, w, ALU.mult))
                    link(dve.tensor_reduce(red[:, 26:28], out, AX.X, ALU.max))
                    link(tt(out, out, red[:, 26:28].unsqueeze(2).broadcast_to([P, 2, n]),
                            ALU.is_equal))

                falling = C("xb")
                gm = red[:, 16:24].rearrange("p (a g) -> p a g", a=2)
                first_max(gm, gs, N_GROUPS, falling[:, 0:4])
                link(ts(red[:, 8:16], red[:, 16:24], -1.0, ALU.add, BIG, ALU.mult))
                gm4 = red[:, 16:24].unsqueeze(2).broadcast_to([P, 8, 4])
                gb4 = red[:, 8:16].unsqueeze(2).broadcast_to([P, 8, 4])
                link(tt(s4, s4, gm4, ALU.mult))
                link(tt(s4, s4, gb4, ALU.add))
                first_max(oh1, sel_, N_EXPERTS, falling[:, 0:16])
                link(stt(sel_, oh1, -4.0 * BIG, sel_, ALU.mult, ALU.add))
                first_max(oh2, sel_, N_EXPERTS, falling[:, 0:16])
                link(tt(oh1, oh1, oh2, ALU.add))
                link(tt(tmp_, oh1, e_, ALU.mult))
                link(dve.tensor_reduce(red[:, 2:4], tmp_, AX.X, ALU.add))
                link(dve.reciprocal(red[:, 4:6], red[:, 2:4]))
                link(tt(tmp_, tmp_, per_token(red[:, 4:6]), ALU.mult))
                ts(rt[:, 11, :, :], tmp_, 0.5, ALU.mult).then_inc(s_gate_ready, 1)
                dve.wait_ge(s_gates_turned, layer + 1)
                link(dve.tensor_copy(gt[:, :], bank[5][0:16, 0:TOK]))
                dve.sem_inc(s_bank_free[5], 1)
                dve.sem_inc(s_gt_ready, 1)
                for e in range(N_EXPERTS):
                    for f in range(4):
                        n = 4 * e + f
                        b = 4 + n % 3
                        dve.wait_ge(s_ff_tanh, 64 * layer + n + 1)
                        if N_EXPERTS * layer + e - 1 > 0:
                            dve.wait_ge(s_expert_done, N_EXPERTS * layer + e - 1)
                        link(stt(sact[:, n % 2, :], th[:, n % 2, :], 1.0, bank[b][:, 0:TOK], ALU.add,
                                 ALU.mult))
                        link(tt(sact[:, n % 2, :], sact[:, n % 2, :], bank[b][:, TOK:2 * TOK],
                                ALU.mult))
                        dve.sem_inc(s_bank_free[b], 1)
                        if f == 0:
                            dve.wait_ge(s_gate_wide, N_EXPERTS * layer + e + 1)
                        link(tt(act[:, 4 * (e % 2) + f, :], sact[:, n % 2, :], bank[7][:, 0:TOK],
                                ALU.mult))
                        dve.sem_inc(s_act_ready, 1)
                    dve.sem_inc(s_bank_free[7], 1)
                dve.wait_ge(s_expert_done, N_EXPERTS * (layer + 1))
                for b in range(4):
                    src = tiles(b)
                    for c in range(2):
                        t = 2 * b + c
                        for g in range(GROUPS):
                            link(stt(x[:, t, g_cols(g)], src[:, c, g_cols(g)],
                                     modT[:, 40 + t, g:g + 1], x[:, t, g_cols(g)], ALU.mult, ALU.add))
                    dve.sem_inc(s_bank_free[b], 1)
                    dve.sem_inc(s_x_moe, 1)
            norm(2 * DEPTH, None)
            dve.sem_inc(s_y_ready, 1)


def lay_out(a):
    def blocks(w, c0, width):
        k = w.shape[0] // P
        return w[:, c0:c0 + width].reshape(k, P, width).transpose(1, 0, 2).reshape(P, k * width)

    pieces = []
    for l in range(DEPTH):
        pieces += [blocks(a["w_ada"][l], c, 256) for c in range(0, 6 * D, 256)]
        pieces += [blocks(a["w_in"][l], c, 256) for c in W_IN_ORDER]
        pieces += [blocks(a["w_gate"][l], c, 256) for c in range(0, 3 * D, 256)]
        for half in range(2):
            pieces += [blocks(a[n][l], 512 * half, 512) for n in ("w_branch_b", "w_branch_c", "w_branch_a")]
        pieces += [blocks(a["w_out"][l], c, 256) for c in range(0, D, 256)]

        def second(e):
            return [blocks(a["moe_w2"][l, e], c, 512) for c in (0, 512)]

        for e in range(N_EXPERTS):
            for c in (0, 256):
                pieces += [blocks(a["moe_w1"][l, e], c, 256), blocks(a["moe_w3"][l, e], c, 256)]
            if e:
                pieces += second(e - 1)
        pieces += second(N_EXPERTS - 1)
    weights = np.stack(pieces)

    def rows(v):
        return v.reshape(-1, P).T

    params = np.zeros((DEPTH, P, N_PAR), np.float32)
    for l in range(DEPTH):
        def put(name, v):
            params[l, :v.shape[0], PAR[name][0]:PAR[name][1]] = v

        put("b_ada", rows(a["b_ada"][l]))
        put("norm1", rows(a["norm1_g"][l]))
        put("norm2", rows(a["norm2_g"][l]))
        put("conv_w", rows(a["hy_conv_w"][l]))
        put("conv_b", rows(a["hy_conv_b"][l]))
        put("skip", rows(a["hy_skip"][l]))
        put("b_gate", rows(a["b_gate"][l]))
        put("subln", rows(a["attn_subln_g"][l]))
        put("lam", np.broadcast_to(a["attn_lambda"][l].reshape(1, -1), (P, 4 * DH_A)))
        r = a["ret_decay_exp"][l]
        put("rde", np.broadcast_to(r.reshape(1, -1), (P, 2 * H_C)))
        put("rde_q", np.repeat(r.reshape(2, 2, 2).transpose(2, 1, 0).reshape(2, 4), 64, axis=0))
        put("f_w1", a["hy_f_w1"][l])
        put("f_b1", a["hy_f_b1"][l].reshape(-1, 1))
        put("f_w2", a["hy_f_w2"][l])
        put("f_b2", a["hy_f_b2"][l].reshape(-1, 1))
        put("f_w3", a["hy_f_w3"][l])
    shared = np.zeros((P, N_SHD), np.float32)
    shared[:, SHD["final"][0]:SHD["final"][1]] = rows(a["final_g"])
    shared[:, SHD["router"][0]:SHD["router"][1]] = blocks(a["w_router"], 0, N_EXPERTS)
    shared[:, SHD["b_router"][0]:SHD["b_router"][1]] = np.broadcast_to(a["b_router"].reshape(1, -1), (P, 16))
    shared[:, SHD["cond"][0]:SHD["cond"][1]] = np.stack([rows(a["c_ctx"]), rows(a["c"][0])], -1).reshape(P, 16)
    x = np.concatenate([a["x_prompt"][0], a["x_sample"][0]], 0)
    x_in = x.T.reshape(KT, P, TOK).transpose(1, 0, 2)
    k_cache = a["cache_attn_k"][0].transpose(0, 3, 2, 1)
    v_cache = a["cache_attn_v"][0].reshape(DEPTH, SEQ, H_A * DV_A)
    s = a["state_retention"][0]
    s_cache = np.zeros((DEPTH, P, H_C, 2, DV_C), np.float32)
    for hh in range(H_C):
        r = 64 * (hh % 2)
        s_cache[:, r:r + 64, hh] = s[:, :, hh].transpose(0, 2, 1, 3)
    out = dict(weights=weights, params=params, consts=constant_columns(), shared=shared, x_in=x_in,
               k_cache=k_cache, v_cache=v_cache, s_cache=s_cache)
    return {n: np.ascontiguousarray(v) for n, v in out.items()}


_OUTS = [("y_out", (P, KT, TOK)), ("k_out", (DEPTH, P, H_A, SEQ)), ("v_out", (DEPTH, SEQ, H_A * DV_A)),
         ("s_out", (DEPTH, 2, DK_C, H_C * DV_C))]


def kernel(**inputs):
    import concourse.bacc as _bacc
    from concourse.bass_utils import run_bass_kernel_spmd as _run

    nc = _bacc.Bacc("TRN2", target_bir_lowering=False, num_devices=1)
    data = lay_out({n: np.asarray(v) for n, v in inputs.items()})
    arrays, args = {}, []
    for name, a in data.items():
        arrays[f"in_{name}"] = a
        args.append(nc.dram_tensor(f"in_{name}", a.shape, F32, kind="ExternalInput").ap())
    for name, shape in _OUTS:
        args.append(nc.dram_tensor(name, shape, F32, kind="ExternalOutput").ap())
    trunk_program(nc, *args)
    r = _run(nc, [arrays], core_ids=[0]).results[0]
    y = r["y_out"].transpose(2, 1, 0).reshape(GROUPS, 1, SEQ, D)
    new_k = r["k_out"].transpose(0, 3, 2, 1)[None]
    new_v = r["v_out"].reshape(1, DEPTH, SEQ, H_A, DV_A)
    new_s = r["s_out"].reshape(DEPTH, 2, DK_C, H_C, DV_C).transpose(0, 1, 3, 2, 4)[None]
    return y[0], y[1], new_k, new_v, new_s
```

```python
import math
from contextlib import ExitStack

import numpy as np
import concourse.bass as bass
from concourse import mybir

F32 = mybir.dt.float32
ALU = mybir.AluOpType
ACT = mybir.ActivationFunctionType
AX = mybir.AxisListType

P = 128
D = 1024
DEPTH = 2
SEQ = 128
GROUPS = 2
TOK = GROUPS * SEQ
KT = D // P
EPS = 1e-6
GRID_W = 64
ROPE_BASE = 10000.0
H_A, DH_A, DV_A = 4, 64, 128
C_B = 512
SHORT_K = 3
H_EMB, H_FFN = 33, 64
H_C, DK_C, DV_C = 4, 64, 128
N_EXPERTS, N_GROUPS, EPG = 16, 4, 4
D_FF = 512
PAIRS = N_EXPERTS // 2
BLOCK = 64
MORE = 2 * TOK // (BLOCK + 1)
OVER = (TOK - 1) // BLOCK
BIG = 1.0e30
TWO_PI_HI = 6.28125
TWO_PI_LO = 2.0 * math.pi - 6.28125
ROUND = 12582912.0
SIN_EDGE = 3.1415925

PIECE = 2048
SLOTS = 8
W_IN_ORDER = [1536 + 256 * i for i in range(6)] + [3072, 3328, 3584, 3840, 0, 256, 512, 768,
                                                   1024, 1280, 4096, 4352]
U_HY, U_QR, U_KR, U_VR, U_QA, U_KA, U_VA, U_GR, U_GATE, U_MERGE, U_OUT = (
    0, 6, 7, 8, 10, 12, 14, 16, 18, 30, 42)
N_PROJ = 46
DENSE_PIECES = 64
PIECES = DENSE_PIECES + 6 * N_EXPERTS


def lam_init(layer):
    return 0.8 - 0.6 * math.exp(-0.3 * layer)


def columns(*parts):
    at, out = 0, {}
    for name, n in parts:
        out[name] = (at, at + n)
        at += n
    return out, at


PAR, N_PAR = columns(("b_ada", 48), ("norm1", 8), ("norm2", 8), ("conv_w", 36), ("conv_b", 12),
                     ("skip", 4), ("b_gate", 24), ("subln", 1), ("lam", 256), ("rde", 8),
                     ("rde_q", 4), ("f_w1", 64), ("f_b1", 1), ("f_w2", 64), ("f_b2", 1),
                     ("f_w3", 1024))
CST, N_CST = columns(("ident", 128), ("rot", 128), ("cos", 128), ("sin", 128), ("cf", 128),
                     ("sf", 128), ("s0", 128), ("nq", 128), ("cf1", 128), ("s1", 128),
                     ("nq1", 128), ("ic", 128), ("is", 128), ("z", 128), ("decay", 512),
                     ("xf", 128), ("xb", 128), ("df", 128), ("db", 128), ("mf", 128),
                     ("mb", 128), ("zf", 1), ("zb", 1))
SHD, N_SHD = columns(("final", 8), ("router", 128), ("b_router", 16), ("cond", 16))


def constant_columns():
    c = np.zeros((P, N_CST), np.float64)

    def put(name, a):
        a = np.asarray(a)
        c[:a.shape[0], CST[name][0]:CST[name][1]] = a

    i = np.arange(P)
    put("ident", np.eye(P))
    rot = np.zeros((P, P))
    q = DH_A // 4
    for b in range(0, P, 2 * q):
        for j in range(q):
            rot[b + q + j, b + j] = -1.0
            rot[b + j, b + q + j] = 1.0
    put("rot", rot)
    inv = (np.float32(ROPE_BASE) ** (-np.arange(q, dtype=np.float32) / np.float32(q)))
    row, col = (i // GRID_W).astype(np.float32), (i % GRID_W).astype(np.float32)
    ar, ac = row[:, None] * inv, col[:, None] * inv
    ang = np.concatenate([ar, ar, ac, ac], -1)
    put("cos", np.tile(np.cos(ang), (1, 2)).T)
    put("sin", np.tile(np.sin(ang), (1, 2)).T)
    w = 2 * np.pi * np.outer(i, i) / (2 * SEQ)
    alt = (-1.0) ** i
    cf, sf, s0, nq = np.cos(w), -np.sin(w), -np.sin(w), np.cos(w)
    sf[:, 0] = alt
    s0[:, 0] = 0.0
    nq[:, 0] = alt
    cf1, nq1 = cf.copy(), nq.copy()
    cf1[0] = nq1[0] = 0.0
    for name, a in (("cf", cf), ("sf", sf), ("s0", s0), ("nq", nq), ("cf1", cf1), ("s1", -s0),
                    ("nq1", nq1)):
        put(name, a)
    ic, isn = 2 * np.cos(w) / (2 * SEQ), -2 * np.sin(w) / (2 * SEQ)
    ic[0] = 1.0 / (2 * SEQ)
    isn[0] = alt / (2 * SEQ)
    put("ic", ic)
    put("is", isn)
    t = np.linspace(0.0, 1.0, SEQ, dtype=np.float32)[:, None]
    bands = (H_EMB - 1) // 2
    wt = (np.float32(2.0 * math.pi) * np.arange(SEQ, dtype=np.float32)[:, None] / np.float32(SEQ))
    fr = np.linspace(1e-4, bands - 1, bands, dtype=np.float32)
    a = wt * fr
    put("z", np.concatenate([t, np.cos(a), -np.sin(a)], -1).T)
    deltas = np.linspace(math.log(1e-2) / 1.5, math.log(1e-2) / 0.3, C_B, dtype=np.float32)
    put("decay", np.exp(-t * np.abs(deltas)))
    one = np.ones((P, 1))
    put("xf", one * (i + 1)[None])
    put("xb", one * (SEQ - i)[None])
    d = i[None, :] - i[:, None]
    put("df", np.maximum(d, 0))
    put("db", np.maximum(-d, 0))
    put("mf", d >= 0)
    put("mb", d <= 0)
    put("zf", (SEQ - 1 - i)[:, None])
    put("zb", i[:, None])
    return c.astype(np.float32)


def trunk_program(nc, weights, experts, params, consts, shared, x_in, k_cache, v_cache, s_cache,
                  y_out, k_out, v_out, s_out):
    with ExitStack() as ctx:
        def sem(name):
            return ctx.enter_context(nc.semaphore(name))

        s_act_ready = sem("act_ready")
        s_more_in = [sem(f"more_in{n}") for n in range(2)]
        s_chosen = sem("chosen")
        s_ranked = sem("ranked")
        s_tokens_turned = sem("tokens_turned")
        s_tokens_copied = sem("tokens_copied")
        s_tokens_copied_s = sem("tokens_copied_s")
        s_picks = sem("picks")
        s_scat_sum = sem("scat_sum")
        s_scat_ready = sem("scat_ready")
        s_gathered = sem("gathered")
        s_hgat_lo = sem("hgat_lo")
        s_hgat_hi = sem("hgat_hi")
        s_act_turned = sem("act_turned")
        s_actT_ready = sem("actT_ready")
        s_y_sum = sem("y_sum")
        s_y_lo = sem("y_lo")
        s_y_hi = sem("y_hi")
        s_combined = sem("combined")
        s_experts_done = sem("experts_done")
        s_more_known = sem("more_known")
        s_more_picked = sem("more_picked")
        s_more_used = sem("more_used")
        s_more_gathered = sem("more_gathered")
        s_more_hgat = sem("more_hgat")
        s_more_ff = sem("more_ff")
        s_more_tanh = sem("more_tanh")
        s_more_act = sem("more_act")
        s_more_turned = sem("more_turned")
        s_more_actT = sem("more_actT")
        s_more_ysum = sem("more_ysum")
        s_more_y = sem("more_y")
        s_more_combined = sem("more_combined")
        s_mod_rows = sem("mod_rows")
        s_mod_rows_copied = sem("mod_rows_copied")
        s_cond_zero = sem("cond_zero")
        s_probs_ready = sem("probs_ready")
        s_amixT_ready = sem("amixT_ready")
        s_amix_ready = sem("amix_ready")
        s_att_out = sem("att_out")
        s_att_scores = sem("att_scores")
        s_att_turned = sem("att_turned")
        s_attr_ready = sem("attr_ready")
        s_b_half = sem("b_half")
        s_bank_free = [sem(f"bank_free{b}") for b in range(8)]
        s_cache_in = sem("cache_in")
        s_cond_ready = sem("cond_ready")
        s_cond_tanh = sem("cond_tanh")
        s_consts_in = sem("consts_in")
        s_conv_mid = sem("conv_mid")
        s_decay_exp = sem("decay_exp")
        s_decay_ln = sem("decay_ln")
        s_decay_log = sem("decay_log")
        s_decay_one = sem("decay_one")
        s_dft_done = sem("dft_done")
        s_ff_sum = sem("ff_sum")
        s_ff_tanh = sem("ff_tanh")
        s_gr_tanh = sem("gr_tanh")
        s_h_ready_s = sem("h_ready_s")
        s_h_ready_v = sem("h_ready_v")
        s_h_scaled = sem("h_scaled")
        s_hid = [sem(f"hid{n}") for n in range(3)]
        s_hid_arg = sem("hid_arg")
        s_hid_sum = sem("hid_sum")
        s_idft_done = sem("idft_done")
        s_ktok_sum = sem("ktok_sum")
        s_kz_ready = sem("kz_ready")
        s_lam_exp = sem("lam_exp")
        s_lam_sums = sem("lam_sums")
        s_logits = sem("logits")
        s_logits_exp = sem("logits_exp")
        s_logits_shifted = sem("logits_shifted")
        s_max_ready = sem("max_ready")
        s_merged = sem("merged")
        s_mod_ready = sem("mod_ready")
        s_mod_sum = sem("mod_sum")
        s_norm_mean = sem("norm_mean")
        s_norm_root = sem("norm_root")
        s_norm_sum = sem("norm_sum")
        s_o_mean = sem("o_mean")
        s_o_norm_sum = sem("o_norm_sum")
        s_o_root = sem("o_root")
        s_o_sum = sem("o_sum")
        s_ones_set = sem("ones_set")
        s_osq_ready = sem("osq_ready")
        s_params_in = sem("params_in")
        s_params_used = sem("params_used")
        s_proj_done = sem("proj_done")
        s_qa_copied = sem("qa_copied")
        s_qa_roped = sem("qa_roped")
        s_qkr_copied = sem("qkr_copied")
        s_qkr_roped = sem("qkr_roped")
        s_qx_ready = sem("qx_ready")
        s_ret_scores = sem("ret_scores")
        s_rotated = sem("rotated")
        s_scalar_link = sem("scalar_link")
        s_shared_in = sem("shared_in")
        s_spectrum_sum = sem("spectrum_sum")
        s_state_copied = sem("state_copied")
        s_state_sum = sem("state_sum")
        s_stored = sem("stored")
        s_stores_read = sem("stores_read")
        s_tables_exp = sem("tables_exp")
        s_taps = sem("taps")
        s_taps_abs = sem("taps_abs")
        s_taps_decayed = sem("taps_decayed")
        s_taps_norm = sem("taps_norm")
        s_taps_sum = sem("taps_sum")
        s_va_copied = sem("va_copied")
        s_vector_link = sem("vector_link")
        s_vr_copied = sem("vr_copied")
        s_weights_in = [sem(f"weights_in{slot}") for slot in range(SLOTS)]
        s_weights_used = sem("weights_used")
        s_x_in = sem("x_in")
        s_x_mixed = sem("x_mixed")
        s_x_moe = sem("x_moe")
        s_x_squared = sem("x_squared")
        s_y_ready = sem("y_ready")
        s_ya_ready = sem("ya_ready")
        s_yb_ready = sem("yb_ready")
        s_yc_ready = sem("yc_ready")
        s_ysp_ready = sem("ysp_ready")
        s_z_ready = sem("z_ready")
        s_zeros_set = sem("zeros_set")
        s_zt_ready = sem("zt_ready")
        s_zt_sum = sem("zt_sum")

        def sb(name, *shape):
            return ctx.enter_context(nc.sbuf_tensor(name, list(shape), F32))

        ring = sb("ring", P, SLOTS, PIECE)
        cst = sb("cst", P, N_CST)
        shd = sb("shd", P, N_SHD)
        par = sb("par", P, N_PAR)
        x = sb("x", P, KT, TOK)
        h = sb("h", P, KT, TOK)
        gates = sb("gates", P, 24, TOK)
        uc = sb("uc", P, 12, TOK)
        qk = sb("qk", P, 8, TOK)
        mix = sb("mix", P, 8, TOK)
        qkr = mix[:, 0:4, :]
        va = sb("va", P, GROUPS, 512)
        vr = sb("vr", P, GROUPS, 512)
        gr = mix[:, 4:8, :]
        kc = sb("kc", P, H_A, SEQ)
        vc = sb("vc", P, H_A * DV_A)
        sc = sb("sc", P, H_C, 2, DV_C)
        filt = sb("filt", P, 3, C_B)
        zt = sb("zt", P, C_B)
        ysp = sb("ysp", P, 2, C_B)
        tmp = sb("tmp", P, C_B)
        attr = sb("attr", P, H_C, SEQ)
        qx = sb("qx", P, 2, 2, SEQ)
        dsum = sb("dsum", P, H_C, SEQ)
        xi = sb("xi", P, 2, 2, SEQ)
        probs = sb("probs", P, 2, 2, 2 * SEQ)
        amix = sb("amix", P, 2, 2 * SEQ)
        amixT = sb("amixT", P, 2, 2 * SEQ)
        osq = zt
        rinv = sb("rinv", P, C_B)
        rms = sb("rms", P, TOK)
        rmsi = sb("rmsi", P, TOK)
        ones = sb("ones", P, P)
        zeros = sb("zeros", P, P)
        modT = sb("modT", P, 48, 2)
        amp = sb("amp", P, 2, 8, 2)
        condT = sb("condT", P, 8, 32)
        sm = sb("sm", P, 640)
        kz = probs[:, 0, :, :]
        sout = qkr[0:64, :, :].rearrange("p a b -> p (a b)").rearrange("p (a b) -> p a b", a=2)
        ints = ctx.enter_context(nc.sbuf_tensor("ints", [P, 2], mybir.dt.int32))
        cnt = sb("cnt", P, 3, OVER * N_EXPERTS)
        rt = sb("rt", P, 6, 2, N_EXPERTS)
        pair = sb("pair", P, 8, 6)

        lgs, lgu, lgm, zeta, lamv, b_half, subg, neglam = (
            sm[:, 0:12], sm[:, 16:28], sm[:, 32:44], sm[:, 48:56], sm[:, 64:68], sm[:, 72:96],
            sm[:, 100:101], sm[:, 104:105])
        lgd, lgn = sm[:, 112:124], sm[:, 128:140]
        mx, sums, rsum = sm[:, 144:148], sm[:, 152:156], sm[:, 160:164]
        hid = sm[:, 176:304]
        rnd = sm[:, 304:432]
        arg = sm[:, 432:560]
        red = sm[:, 560:592]
        hs = uc[:, 0:4, :].rearrange("p a b -> p (a b)").rearrange("p (a b) -> p a b", a=2)
        habs = uc[:, 4:8, :].rearrange("p a b -> p (a b)").rearrange("p (a b) -> p a b", a=2)
        merged = uc[:, 4:12, :]
        def flat(a):
            return a.rearrange("p a b -> p (a b)")

        htok = flat(gates[:, 0:8, :]).rearrange("p (g n) -> p g n", g=2)
        hgat = flat(gates[:, 8:12, :]).rearrange("p (k s) -> p k s", k=KT)
        th = flat(gates[:, 12:14, :])
        act = flat(gates[:, 14:16, :])
        actT = [flat(gates[:, 16 + 2 * i:18 + 2 * i, :]).rearrange("p (f s) -> p f s", f=4)
                for i in range(2)]
        scat = [gates[:, 20 + i, :] for i in range(3)]
        ysb = flat(uc[:, 0:4, :])
        pick = [uc[:, 4 + i, :].rearrange("p (g s) -> p g s", g=2) for i in range(2)]
        pickg = [uc[:, 6 + i, :].rearrange("p (g s) -> p g s", g=2) for i in range(2)]
        more = [flat(qk[:, :, :]), flat(mix[:, :, :])]

        bank = [ctx.enter_context(nc.psum_tensor(f"bank{b}", [P, 512], F32)) for b in range(8)]

        def C(name, rows=P):
            return cst[0:rows, CST[name][0]:CST[name][1]]

        def R(name, rows=P):
            return par[0:rows, PAR[name][0]:PAR[name][1]]

        def H(name):
            return shd[:, SHD[name][0]:SHD[name][1]]

        ident = C("ident")

        def heads(b, n=4):
            return bank[b][:, 0:n * 128].rearrange("p (a b) -> p a b", a=n)

        def tiles(b):
            return bank[b][:, :].rearrange("p (a b) -> p a b", a=2)

        def g_cols(g):
            return slice(g * SEQ, (g + 1) * SEQ)

        block = ctx.enter_context(nc.Block())

        @block.sync
        def _(sp):
            laps = weights.rearrange("d (l s) p c -> d l s p c", s=SLOTS)
            for layer in range(DEPTH):
                base = layer * PIECES
                if layer == 0:
                    for slot in range(SLOTS):
                        sp.dma_start(ring[:, slot, :], weights[0, slot, :, :]).then_inc(
                            s_weights_in[slot], 16)
                with sp.Fori(0 if layer else 1, laps.shape[1]) as lap:
                    for slot in range(SLOTS):
                        sp.wait_ge(s_weights_used, lap * SLOTS + (base + slot + 1 - SLOTS))
                        sp.dma_start(ring[:, slot, :], laps[layer, bass.ds(lap, 1), slot, :, :].rearrange(
                            "a p c -> (a p) c")).then_inc(s_weights_in[slot], 16)
                n = base + DENSE_PIECES
                for p in range(PAIRS + 1):
                    todo = [(2 * p + c % 2, c // 2) for c in range(8)] if p < PAIRS else []
                    todo += [(2 * p - 2 + c % 2, 4 + c // 2) for c in range(4)] if p else []
                    for e, part in todo:
                        sp.wait_ge(s_weights_used, n - SLOTS + 1)
                        sp.dma_start(ring[:, n % SLOTS, :], experts[layer, e, part]).then_inc(
                            s_weights_in[n % SLOTS], 16)
                        n += 1

        @block.gpsimd
        def _(pool):
            pool.dma_start(cst[:, :], consts).then_inc(s_consts_in, 16)
            pool.dma_start(shd[:, :], shared).then_inc(s_shared_in, 16)
            pool.memset(condT[:, :, :], 0.0).then_inc(s_cond_zero, 1)
            pool.memset(ones[:, :], 1.0).then_inc(s_ones_set, 1)
            pool.memset(zeros[:, :], 0.0).then_inc(s_zeros_set, 1)
            for layer in range(DEPTH):
                if layer:
                    pool.wait_ge(s_params_used, layer - 1 + 1)
                pool.dma_start(par[:, :], params[layer, :, :]).then_inc(s_params_in, 16)
                if layer == 0:
                    pool.dma_start(x[:, :, :], x_in).then_inc(s_x_in, 16)
                pool.dma_start(kc[:, :, :], k_cache[layer]).then_inc(s_cache_in, 16)
                pool.dma_start(vc[:, :], v_cache[layer]).then_inc(s_cache_in, 16)
                pool.dma_start(sc[:, :, :, :], s_cache[layer]).then_inc(s_cache_in, 16)
                pool.wait_ge(s_qa_copied, 4 * layer + 4)
                pool.dma_start(k_out[layer], qk[:, 4:8, 0:SEQ]).then_inc(s_stored, 16)
                pool.wait_ge(s_va_copied, 2 * layer + 2)
                pool.dma_start(v_out[layer], va[:, 0, :]).then_inc(s_stored, 16)
                pool.wait_ge(s_state_copied, 2 * layer + 2)
                for way in range(2):
                    pool.dma_start(s_out[layer, way], sout[:, way, :]).then_inc(s_stored, 16)
                pool.wait_ge(s_stored, 16 * 4 * (layer + 1))
                pool.sem_inc(s_stores_read, 1)
            pool.wait_ge(s_y_ready, 1)
            pool.dma_start(y_out, h[:, :, :]).then_inc(s_stored, 16)
            pool.wait_ge(s_stored, 16 * (4 * DEPTH + 1))

        @block.tensor
        def _(pe):
            held = [0] * 8
            pieces = [0]

            def take(b):
                if held[b]:
                    pe.wait_ge(s_bank_free[b], held[b])
                held[b] += 1

            def piece(width):
                n = pieces[0]
                pieces[0] += 1
                pe.wait_ge(s_weights_in[n % SLOTS], 16 * (n // SLOTS + 1))
                return ring[:, n % SLOTS, :].rearrange("p (k n) -> p k n", n=width)

            def then(bank_, event):
                pe.matmul(bank_[0:32, 510:512], zeros[:, 0:32], zeros[:, 0:2], start=False, stop=False,
                          skip_group_check=True).then_inc(event, 1)

            def ada(layer, q):
                w = [piece(256) for _ in range(4)]
                take(q % 2)
                for k in range(KT):
                    for j in range(4):
                        last = pe.matmul(bank[q % 2][32 * j:32 * j + 32, 0:256], condT[:, k, :],
                                         w[j][:, k, :], start=(k == 0), stop=(k == KT - 1),
                                         skip_group_check=True)
                last.then_inc(s_weights_used, 4)
                pe.matmul(bank[q % 2][0:32, 510:512], zeros[:, 0:32], zeros[:, 0:2], start=True,
                          stop=True, skip_group_check=True).then_inc(s_mod_rows, 1)

            def ada_turn(layer, q):
                pe.wait_ge(s_mod_rows_copied, 6 * layer + q + 1)
                take(2 + q % 2)
                for t in range(2):
                    last = pe.transpose(bank[2 + q % 2][:, t * P:(t + 1) * P],
                                        uc[:, 8 + q % 4, t * P:(t + 1) * P], ident)
                last.then_inc(s_mod_sum, 1)

            def filter_step(layer, n):
                if n == 0:
                    pe.wait_ge(s_consts_in, 16)
                    pe.wait_ge(s_params_in, 16 * (layer + 1))
                    take(4)
                    pe.matmul(bank[4][0:64, 0:128], R("f_w1", H_EMB), C("z", H_EMB), start=True,
                              stop=True).then_inc(s_hid_sum, 1)
                elif n == 1:
                    pe.wait_ge(s_hid[1], layer + 1)
                    take(4)
                    pe.matmul(bank[4][0:64, 0:128], R("f_w2", 64), hid[0:64, :], start=True,
                              stop=True).then_inc(s_hid_sum, 1)
                elif n == 2:
                    pe.wait_ge(s_hid[2], layer + 1)
                    for c in range(2):
                        take(4 + c)
                        w3 = R("f_w3", 64)[:, c * 512:(c + 1) * 512]
                        pe.matmul(bank[4 + c][:, :], hid[0:64, :], w3, start=True,
                                  stop=True).then_inc(s_taps_sum, 1)
                elif n == 3:
                    pe.wait_ge(s_taps_abs, layer + 1)
                    take(6)
                    for c in range(2):
                        last = pe.matmul(bank[6][:, :], ones[:, :], habs[:, c, :], start=(c == 0),
                                         stop=(c == 1))
                    last.then_inc(s_taps_norm, 1)
                else:
                    pe.wait_ge(s_taps, layer + 1)
                    for b, a0, a1 in ((4, "cf", "cf1"), (5, "s0", "s1"), (6, "nq", "nq1")):
                        take(b)
                        pe.matmul(bank[b][:, :], C(a0), hs[:, 0, :], start=True, stop=False)
                        pe.matmul(bank[b][:, :], C(a1), hs[:, 1, :], start=False,
                                  stop=True).then_inc(s_spectrum_sum, 1)

            def norm_sum(count):
                take(4)
                for k in range(KT):
                    if k % 4 == 0:
                        pe.wait_ge(s_x_squared, 2 * count + k // 4 + 1)
                    last = pe.matmul(bank[4][:, 0:TOK], ones[:, :], h[:, k, :], start=(k == 0),
                                     stop=(k == KT - 1))
                last.then_inc(s_norm_sum, 1)

            def proj(layer, u):
                b = u % 4
                w = piece(256)
                take(b)
                norms = 2 * layer
                if U_VR <= u < U_QA or U_VA <= u < U_GR:
                    for g in range(GROUPS):
                        for k in range(KT):
                            last = pe.matmul(bank[b][:, g * 256:(g + 1) * 256], h[:, k, g_cols(g)],
                                             w[:, k, :], start=(k == 0), stop=(k == KT - 1))
                else:
                    for c in range(2):
                        for k in range(KT):
                            if u == 0 and c == 0:
                                pe.wait_ge(s_h_ready_v, KT * norms + k + 1)
                                pe.wait_ge(s_h_ready_s, KT * norms + k + 1)
                            last = pe.matmul(bank[b][:, c * TOK:(c + 1) * TOK],
                                             w[:, k, c * P:(c + 1) * P], h[:, k, :],
                                             start=(k == 0), stop=(k == KT - 1))
                last.then_inc(s_weights_used, 1)
                then(bank[b], s_proj_done)

            def z_transpose(layer, g):
                pe.wait_ge(s_z_ready, layer + 1)
                take(4)
                for c in range(4):
                    last = pe.transpose(bank[4][:, c * P:(c + 1) * P], uc[:, 8 + c, g_cols(g)], ident)
                last.then_inc(s_zt_sum, 1)

            def rope(layer, n, src, b):
                if n == 0:
                    pe.wait_ge(s_qkr_copied, 2 * layer + 2)
                else:
                    pe.wait_ge(s_qa_copied, 4 * layer + 2 * n)
                take(b)
                pe.matmul(bank[b][:, :], C("rot"), src, start=True, stop=True).then_inc(s_rotated, 1)

            def dft(layer, g):
                pe.wait_ge(s_zt_ready, 2 * layer + g + 1)
                for b, t in ((6, "cf"), (7, "sf")):
                    take(b)
                    pe.matmul(bank[b][:, :], C(t), zt[:, :], start=True, stop=True).then_inc(
                        s_dft_done, 1)

            def idft(layer, g):
                pe.wait_ge(s_ysp_ready, 2 * layer + g + 1)
                take(5)
                for c in range(4):
                    pe.matmul(bank[5][:, c * P:(c + 1) * P], ysp[:, 0, c * P:(c + 1) * P], C("ic"),
                              start=True, stop=False)
                    last = pe.matmul(bank[5][:, c * P:(c + 1) * P], ysp[:, 1, c * P:(c + 1) * P],
                                     C("is"), start=False, stop=True)
                last.then_inc(s_idft_done, 1)

            def ret_scores(layer, g):
                pe.wait_ge(s_qkr_copied, 2 * layer + 2)
                if g:
                    pe.wait_ge(s_qkr_roped, layer + 1)
                for b in (4, 5):
                    take(b)
                for hh in range(H_C):
                    r = slice(64 * (hh % 2), 64 * (hh % 2) + 64)
                    last = pe.matmul(bank[4 + hh % 2][:, (hh // 2) * P:(hh // 2 + 1) * P],
                                     qkr[r, 2 + hh // 2, g_cols(g)], qkr[r, hh // 2, g_cols(g)],
                                     start=True, stop=True)
                last.then_inc(s_ret_scores, 1)

            def ret_out(layer, g):
                pe.wait_ge(s_attr_ready, 2 * layer + g + 1)
                pe.wait_ge(s_vr_copied, 2 * layer + 2)
                take(6)
                for hh in range(H_C):
                    o = bank[6][:, hh * P:(hh + 1) * P]
                    last = pe.matmul(o, vr[:, g, hh * P:(hh + 1) * P], attr[:, hh, :], start=True,
                                     stop=(g == 0))
                    if g:
                        pe.wait_ge(s_qx_ready, layer + 1)
                        pe.wait_ge(s_cache_in, 48 * (layer + 1))
                        for way in range(2):
                            last = pe.matmul(o, sc[:, hh, way, :], qx[:, hh // 2, way, :],
                                             start=False, stop=(way == 1))
                last.then_inc(s_o_sum, 1)

            def k_transpose(layer):
                take(4)
                for t in range(2):
                    last = pe.transpose(bank[4][:, t * P:(t + 1) * P], qkr[:, 2 + t, 0:SEQ], ident)
                last.then_inc(s_ktok_sum, 1)

            def states(layer):
                pe.wait_ge(s_kz_ready, layer + 1)
                for way in range(2):
                    take(4 + way)
                    for hh in range(H_C):
                        last = pe.matmul(bank[4 + way][0:64, hh * P:(hh + 1) * P],
                                         kz[:, way, hh * 64:(hh + 1) * 64],
                                         vr[:, 0, hh * P:(hh + 1) * P], start=True, stop=True)
                    last.then_inc(s_state_sum, 1)

            def o_norm(layer, j):
                pe.wait_ge(s_osq_ready, 4 * layer + j + 1)
                take(7)
                pe.matmul(bank[7][:, :], ones[:, :], osq[:, :], start=True, stop=True).then_inc(
                    s_o_norm_sum, 1)

            def att_scores(layer, i):
                g, hh = i // 4, i % 4
                pe.wait_ge(s_qa_copied, 4 * layer + 4)
                if g:
                    pe.wait_ge(s_qa_roped, 2 * layer + 2)
                    pe.wait_ge(s_cache_in, 48 * (layer + 1))
                for c in range(2):
                    r = slice(64 * c, 64 * c + 64)
                    take(4 + c)
                    q = qk[r, hh, g_cols(g)]
                    if g:
                        pe.matmul(bank[4 + c][:, 0:SEQ], q, kc[r, hh, :], start=True, stop=True)
                    last = pe.matmul(bank[4 + c][:, g * SEQ:(g + 1) * SEQ], q,
                                     qk[r, 4 + hh, g_cols(g)], start=True, stop=True)
                    last.then_inc(s_att_scores, 1)

            def att_turn(layer, i):
                g = i // 4
                pe.wait_ge(s_amix_ready, 8 * layer + i + 1)
                take(7)
                for t in range(g + 1):
                    last = pe.transpose(bank[7][:, t * P:(t + 1) * P],
                                        amix[:, i % 2, t * P:(t + 1) * P], ident)
                last.then_inc(s_att_turned, 1)

            def att_out(layer, i):
                g, hh = i // 4, i % 4
                pe.wait_ge(s_amixT_ready, 8 * layer + i + 1)
                pe.wait_ge(s_va_copied, 2 * layer + 2)
                if hh == 0:
                    take(6)
                cols = slice(hh * P, (hh + 1) * P)
                if g:
                    pe.matmul(bank[6][:, cols], vc[:, cols], amixT[:, i % 2, 0:P], start=True,
                              stop=False)
                last = pe.matmul(bank[6][:, cols], va[:, g, cols], amixT[:, i % 2, g * P:(g + 1) * P],
                                 start=(g == 0), stop=True)
                last.then_inc(s_att_out, 1)
                if hh == 3:
                    then(bank[6], s_o_sum)

            def merge(layer):
                u = U_MERGE
                for half in range(2):
                    for branch, src, event in ((1, uc, s_yb_ready), (2, gr, s_yc_ready),
                                               (0, qk, s_ya_ready)):
                        w = piece(512)
                        pe.wait_ge(event, 2 * layer + 2)
                        for dp in range(2):
                            b = u % 4
                            take(b)
                            for c in range(2):
                                d = 2 * dp + c
                                for k in range(4):
                                    last = pe.matmul(bank[b][:, c * TOK:(c + 1) * TOK],
                                                     w[:, k, d * P:(d + 1) * P], src[:, k, :],
                                                     start=(k == 0), stop=(k == 3))
                            if dp == 0:
                                last.then_inc(s_proj_done, 1)
                            u += 1
                        last.then_inc(s_weights_used, 1)
                        then(bank[b], s_proj_done)

            def out_proj(layer):
                for u in range(U_OUT, N_PROJ):
                    b = u % 4
                    w = piece(256)
                    take(b)
                    for c in range(2):
                        for k in range(KT):
                            if c == 0 and u == U_OUT and k % 2 == 0:
                                pe.wait_ge(s_merged, 4 * layer + k // 2 + 1)
                            last = pe.matmul(bank[b][:, c * TOK:(c + 1) * TOK],
                                             w[:, k, c * P:(c + 1) * P], merged[:, k, :],
                                             start=(k == 0), stop=(k == KT - 1))
                    last.then_inc(s_weights_used, 1)
                    then(bank[b], s_proj_done)

            def route(layer):
                take(5)
                for g in range(GROUPS):
                    for k in range(KT):
                        if g == 0:
                            pe.wait_ge(s_h_ready_v, KT * (2 * layer + 1) + k + 1)
                            pe.wait_ge(s_h_ready_s, KT * (2 * layer + 1) + k + 1)
                        last = pe.matmul(bank[5][:, g * 16:(g + 1) * 16], h[:, k, g_cols(g)],
                                         H("router")[:, k * 16:(k + 1) * 16], start=(k == 0),
                                         stop=(k == KT - 1))
                last.then_inc(s_logits, 1)

            def ranks(layer):
                pe.wait_ge(s_chosen, layer + 1)
                take(5)
                for col, parts in ((0, (("mf", 0),)), (1, (("mf", 1), (None, 0))),
                                   (2, ((None, 0), (None, 1)))):
                    for n, (m, g) in enumerate(parts):
                        last = pe.matmul(bank[5][:, 16 * col:16 * col + 16],
                                         C(m) if m else ones[:, :], rt[:, 3, g, :],
                                         start=(n == 0), stop=(n == len(parts) - 1))
                last.then_inc(s_ranked, 1)

            def tokens_turn(layer):
                for n in range(4):
                    b = (4, 6, 7, 4)[n]
                    take(b)
                    for c in range(4):
                        k = 4 * (n % 2) + c
                        last = pe.transpose(bank[b][:, c * P:(c + 1) * P], h[:, k, g_cols(n // 2)],
                                            ident)
                    last.then_inc(s_tokens_turned, 1)

            def gather(layer, p):
                pe.wait_ge(s_picks, PAIRS * layer + p + 1)
                take(4)
                for g in range(GROUPS):
                    last = pe.transpose(bank[4][:, g_cols(g)], pickg[p % 2][:, g, :], ident)
                last.then_inc(s_scat_sum, 1)
                for half in (1, 0):
                    take(4 + half)
                    for c in range(4):
                        k = 4 * half + c
                        for g in range(GROUPS):
                            if p == 0 and c == 0:
                                pe.wait_ge(s_tokens_copied, 4 * (layer + 1))
                            last = pe.matmul(bank[4 + half][:, c * P:(c + 1) * P],
                                             htok[:, g, k * P:(k + 1) * P], pick[p % 2][:, g, :],
                                             start=(g == 0), stop=(g == 1))
                    last.then_inc(s_gathered, 1)

            def moe_in(layer, p):
                pe.wait_ge(s_hgat_lo, PAIRS * layer + p + 1)
                pe.wait_ge(s_hgat_hi, PAIRS * layer + p + 1)
                for half in range(2):
                    for b in (6, 7):
                        if half == 0:
                            take(b)
                        w = piece(256), piece(256)
                        for k in range(KT):
                            for j in range(2):
                                last = pe.matmul(bank[b][64 * j:64 * j + 64, half * 256:half * 256 + 256],
                                                 hgat[:, k, 64 * j:64 * j + 64], w[j][:, k, :],
                                                 start=(k == 0), stop=(k == KT - 1),
                                                 skip_group_check=True)
                        last.then_inc(s_weights_used, 2)
                then(bank[7], s_ff_sum)

            def act_turn(layer, p):
                pe.wait_ge(s_act_ready, PAIRS * layer + p + 1)
                take(6)
                for f in range(4):
                    last = pe.transpose(bank[6][:, f * P:(f + 1) * P], act[:, f * P:(f + 1) * P], ident)
                last.then_inc(s_act_turned, 1)

            def moe_out(layer, p):
                pe.wait_ge(s_actT_ready, PAIRS * layer + p + 1)
                for half in range(2):
                    w = piece(512), piece(512)
                    take(4 + half)
                    for f in range(4):
                        for j in range(2):
                            last = pe.matmul(bank[4 + half][64 * j:64 * j + 64, :],
                                             actT[p % 2][:, f, 64 * j:64 * j + 64], w[j][:, f, :],
                                             start=(f == 0), stop=(f == 3), skip_group_check=True)
                    last.then_inc(s_weights_used, 2)
                    then(bank[4 + half], s_y_sum)
                combine(s_y_lo, s_y_hi, PAIRS * layer + p + 1, s_scat_ready, scat[p % 3])
                then(bank[0], s_combined)

            def combine(lo, hi, count, scat_event, matrix):
                pe.wait_ge(scat_event, count)
                for dt in range(KT):
                    if dt == 0:
                        pe.wait_ge(lo, count)
                    if dt == 4:
                        pe.wait_ge(hi, count)
                    pe.matmul(bank[dt // 2][:, (dt % 2) * TOK:(dt % 2 + 1) * TOK],
                              ysb[:, dt * P:(dt + 1) * P], matrix, start=False, stop=False,
                              skip_group_check=True)

            def more_block(layer, i):
                n = MORE * layer + i

                def loaded(part):
                    pe.wait_ge(s_more_in[part % 2], 16 * (3 * n + part // 2 + 1))
                    return more[part % 2]

                pe.wait_ge(s_more_picked, n + 1)
                for g in range(GROUPS):
                    pe.transpose(bank[6][:, g_cols(g)], pickg[0][:, g, :], ident)
                for k in range(KT):
                    for g in range(GROUPS):
                        pe.matmul(bank[4 + k // 4][:, (k % 4) * P:(k % 4 + 1) * P],
                                  htok[:, g, k * P:(k + 1) * P], pick[0][:, g, :],
                                  start=(g == 0), stop=(g == 1))
                then(bank[5], s_more_gathered)
                pe.wait_ge(s_more_hgat, n + 1)
                for part in range(4):
                    w = loaded(part).rearrange("p (k n) -> p k n", n=256)
                    cols = slice(256 * (part // 2), 256 * (part // 2) + 256)
                    for k in range(KT):
                        last = pe.matmul(bank[6 + part % 2][:, cols], hgat[:, k, :], w[:, k, :],
                                         start=(k == 0), stop=(k == KT - 1))
                    last.then_inc(s_more_used, 1)
                then(bank[7], s_more_ff)
                pe.wait_ge(s_more_act, n + 1)
                for f in range(4):
                    last = pe.transpose(bank[4][:, f * P:(f + 1) * P], act[:, f * P:(f + 1) * P], ident)
                last.then_inc(s_more_turned, 1)
                pe.wait_ge(s_more_actT, n + 1)
                for part in range(4, 6):
                    w = loaded(part).rearrange("p (f n) -> p f n", n=512)
                    for f in range(4):
                        last = pe.matmul(bank[2 + part][:, :], actT[0][:, f, :], w[:, f, :],
                                         start=(f == 0), stop=(f == 3))
                    last.then_inc(s_more_used, 1)
                then(bank[7], s_more_ysum)
                combine(s_more_y, s_more_y, n + 1, s_more_y, scat[0])
                then(bank[0], s_more_combined)

            pe.wait_ge(s_cond_ready, 1)
            pe.wait_ge(s_ones_set, 1)
            pe.wait_ge(s_zeros_set, 1)
            for layer in range(DEPTH):
                for q in range(6):
                    ada(layer, q)
                    if q < 5:
                        filter_step(layer, q)
                    else:
                        norm_sum(2 * layer)
                    if q:
                        ada_turn(layer, q - 1)
                ada_turn(layer, 5)
                for u in range(U_MERGE):
                    proj(layer, u)
                    if u == 7:
                        z_transpose(layer, 0)
                    if u == 8:
                        rope(layer, 0, qkr[:, :, SEQ:TOK], 5)
                    if u == 9:
                        dft(layer, 0)
                    if u == 10:
                        z_transpose(layer, 1)
                    if u == 11:
                        ret_scores(layer, 0)
                    if u == 12:
                        dft(layer, 1)
                    if u == 13:
                        idft(layer, 0)
                        rope(layer, 1, qk[:, 0:4, SEQ:TOK], 4)
                    if u == 14:
                        rope(layer, 2, qk[:, 4:8, SEQ:TOK], 4)
                        ret_out(layer, 0)
                    if u == 15:
                        idft(layer, 1)
                        o_norm(layer, 0)
                    if u == 16:
                        ret_scores(layer, 1)
                    if u == 17:
                        k_transpose(layer)
                        ret_out(layer, 1)
                    if u == 18:
                        o_norm(layer, 1)
                        states(layer)
                    if 19 <= u < 29:
                        i = u - 19
                        if i < 8:
                            att_scores(layer, i)
                        if 1 <= i < 9:
                            att_turn(layer, i - 1)
                        if i >= 2:
                            att_out(layer, i - 2)
                            if i - 2 == 3:
                                o_norm(layer, 2)
                    if u == 29:
                        o_norm(layer, 3)
                merge(layer)
                out_proj(layer)
                norm_sum(2 * layer + 1)
                route(layer)
                tokens_turn(layer)
                ranks(layer)
                for b in range(4):
                    take(b)
                    pe.matmul(bank[b][:, :], zeros[:, :], h[:, 0:2, :], start=True, stop=False,
                              skip_group_check=True)
                gather(layer, 0)
                for p in range(PAIRS):
                    moe_in(layer, p)
                    if p + 1 < PAIRS:
                        gather(layer, p + 1)
                    act_turn(layer, p)
                    if p:
                        moe_out(layer, p - 1)
                moe_out(layer, PAIRS - 1)
                for b in range(4, 8):
                    take(b)
                pe.wait_ge(s_more_known, layer + 1)
                blocks = pe.value_load(ints[0:1, 0:1], min_val=0, max_val=MORE)
                for i in range(MORE):
                    with pe.If(blocks > i):
                        more_block(layer, i)
                    with pe.Else():
                        for event in (s_more_gathered, s_more_ff, s_more_turned, s_more_ysum,
                                      s_more_combined):
                            if MORE * layer + i:
                                pe.wait_ge(event, MORE * layer + i)
                            pe.sem_inc(event, 1)
                        if MORE * layer + i:
                            pe.wait_ge(s_more_used, 6 * (MORE * layer + i))
                        pe.sem_inc(s_more_used, 6)
                then(bank[0], s_experts_done)
            norm_sum(2 * DEPTH)

        @block.scalar
        def _(act_e):
            sc_e = act_e
            links = [0]

            def link(ins):
                links[0] += 1
                ins.then_inc(s_scalar_link, 1)
                sc_e.wait_ge(s_scalar_link, links[0])

            def squares(count, source, per):
                for half in range(2):
                    if source is s_x_in:
                        sc_e.wait_ge(s_x_in, 16)
                    else:
                        sc_e.wait_ge(source, per + 2 * half + 2)
                    sc_e.activation(h[:, 4 * half:4 * half + 4, :], x[:, 4 * half:4 * half + 4, :],
                                    ACT.Square).then_inc(s_x_squared, 1)

            def norm(count, which):
                sc_e.wait_ge(s_norm_mean, count + 1)
                sc_e.activation(rms[:, :], rmsi[:, :], ACT.Sqrt).then_inc(s_norm_root, 1)
                if which is None:
                    return
                for k in range(KT):
                    sc_e.wait_ge(s_h_scaled, KT * count + k + 1)
                    sc_e.activation(h[:, k, 0:SEQ], h[:, k, 0:SEQ], ACT.Identity,
                                    scale=amp[:, which, k, 0:1],
                                    bias=modT[:, 24 * which + k, 0:1]).then_inc(s_h_ready_s, 1)

            def o_rms(layer, j):
                sc_e.wait_ge(s_o_sum, 4 * layer + j + 1)
                if 4 * layer + j > 0:
                    sc_e.wait_ge(s_o_norm_sum, 4 * layer + j)
                sc_e.activation(osq[:, :], bank[6][:, :], ACT.Square).then_inc(s_osq_ready, 1)
                sc_e.wait_ge(s_o_mean, 4 * layer + j + 1)
                sc_e.activation(tmp[:, :], rinv[:, :], ACT.Sqrt).then_inc(s_o_root, 1)

            sc_e.wait_ge(s_shared_in, 16)
            cond = H("cond").rearrange("p (a b) -> p a b", a=8)
            sc_e.wait_ge(s_cond_zero, 1)
            sc_e.activation(condT[:, :, 0:2], cond, ACT.Tanh, scale=0.5).then_inc(s_cond_tanh, 1)
            for layer in range(DEPTH):
                sc_e.wait_ge(s_consts_in, 16)
                sc_e.wait_ge(s_params_in, 16 * (layer + 1))
                sc_e.activation(lgs[:, :], par[:, PAR["rde"][0]:PAR["rde_q"][1]], ACT.Exp,
                                scale=-math.log(2.0)).then_inc(s_decay_exp, 1)
                sc_e.wait_ge(s_lam_sums, layer + 1)
                sc_e.activation(lamv[:, 2:4], lamv[:, 0:2], ACT.Exp).then_inc(s_lam_exp, 1)
                sc_e.wait_ge(s_decay_one, layer + 1)
                sc_e.activation(lgn[:, :], lgu[:, :], ACT.Ln).then_inc(s_decay_ln, 1)
                sc_e.wait_ge(s_decay_log, layer + 1)
                for t in range(2):
                    for way, name in enumerate(("xf", "xb")):
                        sc_e.activation(xi[:, t, way, :], C(name), ACT.Exp,
                                        scale=lgm[:, 8 + 2 * t + way:9 + 2 * t + way])
                for hh in range(H_C):
                    sc_e.activation(dsum[:, hh, :], C("df"), ACT.Exp, scale=lgm[:, hh:hh + 1])
                    sc_e.activation(attr[:, hh, :], C("db"), ACT.Exp, scale=lgm[:, 4 + hh:5 + hh])
                sc_e.activation(zeta[:, :], zeta[:, :], ACT.Exp).then_inc(s_tables_exp, 1)
                def mod_rows(q):
                    sc_e.wait_ge(s_mod_rows, 6 * layer + q + 1)
                    if 6 * layer + q - 3 > 0:
                        sc_e.wait_ge(s_mod_sum, 6 * layer + q - 3)
                    sc_e.activation(uc[:, 8 + q % 4, :], bank[q % 2][:, 0:256], ACT.Copy).then_inc(
                        s_mod_rows_copied, 1)
                    sc_e.wait_ge(s_mod_rows_copied, 6 * layer + q + 1)
                    sc_e.sem_inc(s_bank_free[q % 2], 1)

                for n in range(2):
                    mod_rows(n)
                    sc_e.wait_ge(s_hid_arg, 2 * layer + n + 1)
                    sc_e.activation(hid[0:64, :], arg[0:64, :], ACT.Sin).then_inc(s_hid[n + 1], 1)
                mod_rows(2)
                sc_e.wait_ge(s_taps_decayed, layer + 1)
                sc_e.activation(habs[:, :, :], hs[:, :, :], ACT.Abs).then_inc(s_taps_abs, 1)
                mod_rows(3)
                mod_rows(4)
                for n in range(3):
                    sc_e.wait_ge(s_spectrum_sum, 3 * layer + n + 1)
                    sc_e.activation(filt[:, n, :], bank[4 + n][:, :], ACT.Copy).then_inc(
                        s_bank_free[4 + n], 1)
                mod_rows(5)
                if layer == 0:
                    squares(0, s_x_in, 0)
                else:
                    squares(2 * layer, s_x_moe, 4 * (layer - 1))
                sc_e.wait_ge(s_mod_ready, layer + 1)
                norm(2 * layer, 0)

                def unit(u):
                    sc_e.wait_ge(s_proj_done, N_PROJ * layer + u + 1)
                    return bank[u % 4], tiles(u % 4), s_bank_free[u % 4]

                for u in range(U_HY, U_HY + 6):
                    _, src, _ = unit(u)
                    for c in range(2):
                        t = 2 * u + c
                        sc_e.activation(uc[:, t, :], src[:, c, :], ACT.Identity,
                                        scale=R("conv_w")[:, 12 + t:13 + t],
                                        bias=R("conv_b")[:, t:t + 1]).then_inc(s_conv_mid, 1)

                def copy_out(u):
                    full, src, free = unit(u)
                    if u in (U_QR, U_KR):
                        if layer and u == U_QR:
                            sc_e.wait_ge(s_stores_read, layer)
                        sc_e.activation(qkr[:, 2 * (u - U_QR):2 * (u - U_QR) + 2, :], src, ACT.Copy,
                                        scale=1.0 if u == U_QR else DK_C ** -0.5).then_inc(
                                            s_qkr_copied, 1)
                        event, done = s_qkr_copied, 2 * layer + u - U_QR + 1
                    elif u < U_QA:
                        sc_e.activation(vr[:, :, 256 * (u - U_VR):256 * (u - U_VR) + 256], src,
                                        ACT.Copy).then_inc(s_vr_copied, 1)
                        event, done = s_vr_copied, 2 * layer + u - U_VR + 1
                    elif u < U_VA:
                        t = 2 * (u - U_QA)
                        sc_e.activation(qk[:, t:t + 2, :], src, ACT.Copy).then_inc(s_qa_copied, 1)
                        event, done = s_qa_copied, 4 * layer + u - U_QA + 1
                    else:
                        sc_e.activation(va[:, :, 256 * (u - U_VA):256 * (u - U_VA) + 256], src,
                                        ACT.Copy).then_inc(s_va_copied, 1)
                        event, done = s_va_copied, 2 * layer + u - U_VA + 1
                    sc_e.wait_ge(event, done)
                    sc_e.sem_inc(free, 1)

                def zt_copy(g):
                    sc_e.wait_ge(s_zt_sum, 2 * layer + g + 1)
                    if 2 * (2 * layer + g) > 0:
                        sc_e.wait_ge(s_dft_done, 2 * (2 * layer + g))
                    sc_e.activation(zt[:, :], bank[4][:, :], ACT.Copy).then_inc(s_zt_ready, 1)
                    sc_e.wait_ge(s_zt_ready, 2 * layer + g + 1)
                    sc_e.sem_inc(s_bank_free[4], 1)

                def gate(u):
                    _, src, free = unit(u)
                    if u == U_GATE:
                        sc_e.wait_ge(s_b_half, layer + 1)
                    for c in range(2):
                        t = 2 * (u - U_GATE) + c
                        last = sc_e.activation(gates[:, t, :], src[:, c, :], ACT.Tanh, scale=0.5,
                                               bias=b_half[:, t:t + 1])
                    last.then_inc(free, 1)

                def softmax(i):
                    g = i // 4
                    n = 128 * (g + 1)
                    sc_e.wait_ge(s_max_ready, 8 * layer + i + 1)
                    if 8 * layer + i - 1 > 0:
                        sc_e.wait_ge(s_amix_ready, 8 * layer + i - 1)
                    for c in range(2):
                        sc_e.activation(probs[:, i % 2, c, 0:n], bank[4 + c][:, 0:n], ACT.Exp,
                                        scale=DH_A ** -0.5, bias=mx[:, 2 + c:3 + c],
                                        accum_out=sums[:, c:c + 1]).then_inc(s_probs_ready, 1)
                    sc_e.wait_ge(s_probs_ready, 16 * layer + 2 * i + 2)
                    for c in range(2):
                        sc_e.sem_inc(s_bank_free[4 + c], 1)

                def turn_copy(i):
                    g = i // 4
                    n = 128 * (g + 1)
                    sc_e.wait_ge(s_att_turned, 8 * layer + i + 1)
                    if 8 * layer + i - 1 > 0:
                        sc_e.wait_ge(s_att_out, 8 * layer + i - 1)
                    sc_e.activation(amixT[:, i % 2, 0:n], bank[7][:, 0:n], ACT.Copy).then_inc(
                        s_amixT_ready, 1)
                    sc_e.wait_ge(s_amixT_ready, 8 * layer + i + 1)
                    sc_e.sem_inc(s_bank_free[7], 1)

                def state_copy():
                    for way in range(2):
                        sc_e.wait_ge(s_state_sum, 2 * layer + way + 1)
                        sc_e.activation(sout[:, way, :], bank[4 + way][0:64, :], ACT.Copy).then_inc(
                            s_state_copied, 1)
                        sc_e.wait_ge(s_state_copied, 2 * layer + way + 1)
                        sc_e.sem_inc(s_bank_free[4 + way], 1)

                copy_out(6)
                copy_out(7)
                zt_copy(0)
                for u in (8, 9, 10):
                    copy_out(u)
                zt_copy(1)
                for u in (11, 12, 13, 14):
                    copy_out(u)
                o_rms(layer, 0)
                copy_out(15)
                for u in (16, 17):
                    _, src, _ = unit(u)
                    t = 2 * (u - U_GR)
                    sc_e.activation(gr[:, t:t + 2, :], src, ACT.Tanh, scale=0.5).then_inc(
                        s_gr_tanh, 1)
                o_rms(layer, 1)
                gate(18)
                state_copy()
                for u in range(19, 30):
                    gate(u)
                    i = u - 19
                    if i < 8:
                        softmax(i)
                    if 1 <= i < 9:
                        turn_copy(i - 1)
                    if i - 2 == 3:
                        o_rms(layer, 2)
                    if i - 2 == 7:
                        o_rms(layer, 3)
                squares(2 * layer + 1, s_x_mixed, 4 * layer)
                norm(2 * layer + 1, 1)
                sc_e.wait_ge(s_logits_shifted, layer + 1)
                sc_e.activation(rt[:, 0, :, :], rt[:, 0, :, :], ACT.Exp).then_inc(s_logits_exp, 1)
                for n in (1, 3):
                    sc_e.wait_ge(s_tokens_turned, 4 * layer + n + 1)
                    b = (4, 6, 7, 4)[n]
                    sc_e.activation(htok[:, n // 2, 512:1024], bank[b][:, :], ACT.Copy).then_inc(
                        s_tokens_copied_s, 1)
                    sc_e.wait_ge(s_tokens_copied_s, 2 * layer + (n + 1) // 2)
                    sc_e.sem_inc(s_bank_free[b], 1)
                    sc_e.sem_inc(s_tokens_copied, 1)

                def gathered(p):
                    n = PAIRS * layer + p
                    sc_e.wait_ge(s_scat_sum, n + 1)
                    sc_e.activation(scat[p % 3], bank[4][:, 0:TOK], ACT.Copy).then_inc(s_scat_ready, 1)
                    sc_e.wait_ge(s_scat_ready, n + 1)
                    sc_e.sem_inc(s_bank_free[4], 1)
                    sc_e.wait_ge(s_gathered, 2 * n + 2)
                    sc_e.activation(flat(hgat[:, 0:4, :]), bank[4][:, :], ACT.Copy).then_inc(
                        s_hgat_lo, 1)
                    sc_e.wait_ge(s_hgat_lo, n + 1)
                    sc_e.sem_inc(s_bank_free[4], 1)

                def out_low(p):
                    n = PAIRS * layer + p
                    sc_e.wait_ge(s_y_sum, 2 * n + 1)
                    if n:
                        sc_e.wait_ge(s_combined, n)
                    sc_e.activation(ysb[:, 0:512], bank[4][:, :], ACT.Copy).then_inc(s_y_lo, 1)
                    sc_e.wait_ge(s_y_lo, n + 1)
                    sc_e.sem_inc(s_bank_free[4], 1)

                gathered(0)
                for p in range(PAIRS):
                    n = PAIRS * layer + p
                    sc_e.wait_ge(s_ff_sum, n + 1)
                    sc_e.activation(th, bank[6][:, :], ACT.Tanh, scale=0.5).then_inc(s_ff_tanh, 1)
                    if p + 1 < PAIRS:
                        gathered(p + 1)
                    sc_e.wait_ge(s_act_turned, n + 1)
                    sc_e.activation(flat(actT[p % 2]), bank[6][:, :], ACT.Copy).then_inc(
                        s_actT_ready, 1)
                    sc_e.wait_ge(s_actT_ready, n + 1)
                    sc_e.sem_inc(s_bank_free[6], 1)
                    if p:
                        out_low(p - 1)
                out_low(PAIRS - 1)
                sc_e.wait_ge(s_more_known, layer + 1)
                sc_e.wait_ge(s_stores_read, layer + 1)
                blocks = sc_e.value_load(ints[0:1, 0:1], min_val=0, max_val=MORE)
                for i in range(MORE):
                    with sc_e.If(blocks > i):
                        sc_e.wait_ge(s_more_picked, MORE * layer + i + 1)
                        e = sc_e.value_load(ints[0:1, 1:2], min_val=0, max_val=N_EXPERTS - 1)
                        for part in range(6):
                            n = 6 * (MORE * layer + i) + part
                            if n >= 2:
                                sc_e.wait_ge(s_more_used, n - 1)
                            sc_e.dma_start(more[part % 2], experts[layer, bass.ds(e, 1), part, :, :]
                                           .rearrange("a p c -> (a p) c")).then_inc(
                                               s_more_in[part % 2], 16)
                        sc_e.wait_ge(s_more_ff, MORE * layer + i + 1)
                        sc_e.activation(th, bank[6][:, :], ACT.Tanh, scale=0.5).then_inc(
                            s_more_tanh, 1)
                    with sc_e.Else():
                        if MORE * layer + i:
                            sc_e.wait_ge(s_more_tanh, MORE * layer + i)
                        sc_e.sem_inc(s_more_tanh, 1)
                        for part in range(2):
                            if MORE * layer + i:
                                sc_e.wait_ge(s_more_in[part], 48 * (MORE * layer + i))
                            sc_e.sem_inc(s_more_in[part], 48)
            squares(2 * DEPTH, s_x_moe, 4 * (DEPTH - 1))
            norm(2 * DEPTH, None)

        @block.vector
        def _(dve):
            links = [0]

            def link(ins):
                links[0] += 1
                ins.then_inc(s_vector_link, 1)
                dve.wait_ge(s_vector_link, links[0])

            def tt(out, a, b, op):
                return dve.tensor_tensor(out, a, b, op)

            def ts(out, a, s1, op0, s2=None, op1=None):
                if op1 is None:
                    return dve.tensor_scalar(out, a, s1, None, op0)
                return dve.tensor_scalar(out, a, s1, s2, op0, op1)

            def stt(out, a, s, b, op0, op1):
                return dve.scalar_tensor_tensor(out, a, s, b, op0, op1)

            def norm(count, which):
                dve.wait_ge(s_norm_sum, count + 1)
                link(ts(rmsi[:, :], bank[4][:, 0:TOK], 1.0 / D, ALU.mult, EPS, ALU.add))
                dve.sem_inc(s_bank_free[4], 1)
                dve.sem_inc(s_norm_mean, 1)
                dve.wait_ge(s_norm_root, count + 1)
                link(dve.reciprocal(rmsi[:, :], rms[:, :]))
                for k in range(KT):
                    tt(h[:, k, :], x[:, k, :], rmsi[:, :], ALU.mult).then_inc(s_h_scaled, 1)
                    dve.wait_ge(s_h_scaled, KT * count + k + 1)
                    if which is None:
                        link(ts(h[:, k, :], h[:, k, :], H("final")[:, k:k + 1], ALU.mult))
                    else:
                        ts(h[:, k, SEQ:TOK], h[:, k, SEQ:TOK], amp[:, which, k, 1:2], ALU.mult,
                           modT[:, 24 * which + k, 1:2], ALU.add).then_inc(s_h_ready_v, 1)

            def sine_arg(layer, n):
                dve.wait_ge(s_hid_sum, 2 * layer + n + 1)
                a, r = arg[0:64, :], rnd[0:64, :]
                link(ts(a, bank[4][0:64, 0:128], R(f"f_b{n + 1}", 64), ALU.add))
                dve.sem_inc(s_bank_free[4], 1)
                link(ts(r, a, 1.0 / (2 * math.pi), ALU.mult, ROUND, ALU.add))
                link(ts(r, r, -ROUND, ALU.add))
                link(stt(a, r, -TWO_PI_HI, a, ALU.mult, ALU.add))
                link(stt(a, r, -TWO_PI_LO, a, ALU.mult, ALU.add))
                ts(a, a, SIN_EDGE, ALU.min, -SIN_EDGE, ALU.max).then_inc(s_hid_arg, 1)

            dve.wait_ge(s_shared_in, 16)
            cond = H("cond").rearrange("p (a b) -> p a b", a=8)
            dve.wait_ge(s_cond_tanh, 1)
            link(stt(condT[:, :, 0:2], condT[:, :, 0:2], 1.0, cond, ALU.add, ALU.mult))
            ts(condT[:, :, 0:2], condT[:, :, 0:2], 0.5, ALU.mult).then_inc(s_cond_ready, 1)

            for layer in range(DEPTH):
                dve.wait_ge(s_consts_in, 16)
                dve.wait_ge(s_params_in, 16 * (layer + 1))
                lam = R("lam").rearrange("p (a b c) -> p a b c", a=2, b=2)
                link(tt(probs[:, 0, :, 0:64], lam[:, :, 0, :], lam[:, :, 1, :], ALU.mult))
                dve.tensor_reduce(lamv[:, 0:2], probs[:, 0, :, 0:64], AX.X, ALU.add).then_inc(
                    s_lam_sums, 1)
                dve.wait_ge(s_lam_exp, layer + 1)
                link(tt(neglam, lamv[:, 3:4], lamv[:, 2:3], ALU.subtract))
                link(ts(neglam, neglam, -lam_init(layer), ALU.add))
                link(ts(subg, R("subln"), 1.0 - lam_init(layer), ALU.mult))
                ts(b_half[:, :], R("b_gate"), 0.5, ALU.mult).then_inc(s_b_half, 1)
                dve.wait_ge(s_decay_exp, layer + 1)
                ts(lgu[:, :], lgs[:, :], -1.0, ALU.mult, 1.0, ALU.add).then_inc(s_decay_one, 1)
                dve.wait_ge(s_decay_ln, layer + 1)
                link(ts(lgd[:, :], lgu[:, :], 1.0, ALU.is_equal))
                link(stt(lgu[:, :], lgu[:, :], -1.0, lgd[:, :], ALU.add, ALU.add))
                link(dve.reciprocal(lgm[:, :], lgu[:, :]))
                link(tt(lgm[:, :], lgm[:, :], lgn[:, :], ALU.mult))
                link(tt(lgm[:, :], lgm[:, :], lgd[:, :], ALU.add))
                link(stt(lgm[:, :], lgs[:, :], -1.0, lgm[:, :], ALU.mult, ALU.mult))
                link(ts(zeta[:, 0:4], lgm[:, 0:4], C("zf"), ALU.mult))
                link(ts(zeta[:, 4:8], lgm[:, 4:8], C("zb"), ALU.mult))
                dve.sem_inc(s_decay_log, 1)
                dve.wait_ge(s_tables_exp, layer + 1)

                def wide(a, n):
                    return a.unsqueeze(1).broadcast_to([P, n, a.shape[-1]])

                link(tt(dsum[:, :, :], dsum[:, :, :], wide(C("mf"), 4), ALU.mult))
                link(tt(attr[:, :, :], attr[:, :, :], wide(C("mb"), 4), ALU.mult))
                link(tt(dsum[:, :, :], dsum[:, :, :], attr[:, :, :], ALU.add))
                sine_arg(layer, 0)
                sine_arg(layer, 1)
                for c in range(2):
                    dve.wait_ge(s_taps_sum, 2 * layer + c + 1)
                    link(tt(hs[:, c, :], bank[4 + c][:, :], C("decay"), ALU.mult))
                    dve.sem_inc(s_bank_free[4 + c], 1)
                dve.sem_inc(s_taps_decayed, 1)
                dve.wait_ge(s_taps_norm, layer + 1)
                link(dve.reciprocal(tmp[:, :], bank[6][:, :]))
                dve.sem_inc(s_bank_free[6], 1)
                link(tt(hs[:, :, :], hs[:, :, :], wide(tmp[:, :], 2), ALU.mult))
                dve.sem_inc(s_taps, 1)
                for q in range(6):
                    dve.wait_ge(s_mod_sum, 6 * layer + q + 1)
                    for t in range(2):
                        src = bank[2 + q % 2][:, t * P:(t + 1) * P].rearrange("p (j c) -> p j c", j=4)
                        link(tt(modT[:, 8 * q + t:8 * q + 8:2, :], src[:, :, 0:2],
                                R("b_ada")[:, 8 * q + t:8 * q + 8:2].unsqueeze(2).broadcast_to(
                                    [P, 4, 2]), ALU.add))
                    dve.sem_inc(s_bank_free[2 + q % 2], 1)
                for n in range(2):
                    link(stt(amp[:, n, :, :], modT[:, 24 * n + 8:24 * n + 16, :], 1.0,
                             R(f"norm{n + 1}").unsqueeze(2).broadcast_to([P, 8, 2]), ALU.add, ALU.mult))
                link(ts(modT[:, 16:24, :], modT[:, 16:24, :], 0.5, ALU.mult))
                dve.sem_inc(s_mod_ready, 1)
                norm(2 * layer, 0)

                def unit(u):
                    dve.wait_ge(s_proj_done, N_PROJ * layer + u + 1)
                    return tiles(u % 4), s_bank_free[u % 4]

                for u in range(U_HY, U_HY + 6):
                    src, free = unit(u)
                    for c in range(2):
                        t = 2 * u + c
                        dve.wait_ge(s_conv_mid, 12 * layer + 2 * u + 2)
                        s = src[:, c, :].rearrange("p (g t) -> p g t", g=2)
                        o = uc[:, t, :].rearrange("p (g t) -> p g t", g=2)
                        link(stt(o[:, :, 1:SEQ], s[:, :, 0:SEQ - 1], R("conv_w")[:, t:t + 1],
                                 o[:, :, 1:SEQ], ALU.mult, ALU.add))
                        link(stt(o[:, :, 0:SEQ - 1], s[:, :, 1:SEQ],
                                 R("conv_w")[:, 24 + t:25 + t], o[:, :, 0:SEQ - 1], ALU.mult, ALU.add))
                    dve.sem_inc(free, 1)
                link(tt(uc[:, 8:12, :], uc[:, 8:12, :], uc[:, 4:8, :], ALU.mult))
                dve.sem_inc(s_z_ready, 1)

                cosw, sinw = wide(C("cos"), 4), wide(C("sin"), 4)

                def rope(n, dst, b, event):
                    dve.wait_ge(s_rotated, 3 * layer + n + 1)
                    tw = tmp[:, :].rearrange("p (a b) -> p a b", a=4)
                    link(tt(tw, heads(b), sinw, ALU.mult))
                    dve.sem_inc(s_bank_free[b], 1)
                    link(tt(dst, dst, cosw, ALU.mult))
                    link(tt(dst, dst, tw, ALU.add))
                    dve.sem_inc(event, 1)

                def spectrum(g):
                    dve.wait_ge(s_dft_done, 4 * layer + 2 * g + 2)
                    if 2 * layer + g > 0:
                        dve.wait_ge(s_idft_done, 2 * layer + g)
                    ur, ui = bank[6][:, :], bank[7][:, :]
                    link(tt(ysp[:, 0, :], ur, filt[:, 0, :], ALU.mult))
                    link(tt(tmp[:, :], ui, filt[:, 1, :], ALU.mult))
                    link(tt(ysp[:, 0, :], ysp[:, 0, :], tmp[:, :], ALU.subtract))
                    link(tt(ysp[:, 1, :], ur, filt[:, 1, :], ALU.mult))
                    dve.sem_inc(s_bank_free[6], 1)
                    link(tt(tmp[:, :], ui, filt[:, 2, :], ALU.mult))
                    dve.sem_inc(s_bank_free[7], 1)
                    link(tt(ysp[:, 1, :], ysp[:, 1, :], tmp[:, :], ALU.add))
                    dve.sem_inc(s_ysp_ready, 1)

                def hyena_out(g):
                    dve.wait_ge(s_idft_done, 2 * layer + g + 1)
                    tw = tmp[:, :].rearrange("p (a b) -> p a b", a=4)
                    for c in range(4):
                        link(stt(tw[:, c, :], uc[:, 8 + c, g_cols(g)], R("skip")[:, c:c + 1],
                                 bank[5][:, c * P:(c + 1) * P], ALU.mult, ALU.add))
                    dve.sem_inc(s_bank_free[5], 1)
                    link(tt(uc[:, 0:4, g_cols(g)], uc[:, 0:4, g_cols(g)], tw, ALU.mult))
                    dve.sem_inc(s_yb_ready, 1)

                def ret_decay(g):
                    dve.wait_ge(s_ret_scores, 2 * layer + g + 1)
                    if 4 * layer + g > 0:
                        dve.wait_ge(s_o_sum, 4 * layer + g)
                    for odd in range(2):
                        link(tt(attr[:, odd::2, :], heads(4 + odd, 2), dsum[:, odd::2, :], ALU.mult))
                        dve.sem_inc(s_bank_free[4 + odd], 1)
                    dve.sem_inc(s_attr_ready, 1)

                def o_scale(j, b=6):
                    dve.wait_ge(s_o_norm_sum, 4 * layer + j + 1)
                    link(ts(rinv[:, :], bank[7][:, :], 1.0 / DV_A, ALU.mult, EPS, ALU.add))
                    dve.sem_inc(s_bank_free[7], 1)
                    dve.sem_inc(s_o_mean, 1)
                    dve.wait_ge(s_o_root, 4 * layer + j + 1)
                    link(dve.reciprocal(rinv[:, :], tmp[:, :]))

                rw = rinv[:, :].rearrange("p (a b) -> p a b", a=4)

                def yc(g):
                    o_scale(g)
                    link(tt(rw, heads(6), rw, ALU.mult))
                    dve.sem_inc(s_bank_free[6], 1)

                def yc_gate(g):
                    link(stt(gr[:, :, g_cols(g)], rw, 0.5, gr[:, :, g_cols(g)], ALU.mult, ALU.mult))
                    dve.sem_inc(s_yc_ready, 1)

                def ya(g):
                    o_scale(2 + g)
                    link(stt(qk[:, 0:4, g_cols(g)], heads(6), subg, rw, ALU.mult, ALU.mult))
                    dve.sem_inc(s_bank_free[6], 1)
                    dve.sem_inc(s_ya_ready, 1)

                def soft_max(i):
                    g = i // 4
                    n = 128 * (g + 1)
                    for c in range(2):
                        dve.wait_ge(s_att_scores, 16 * layer + 2 * i + c + 1)
                        link(dve.tensor_reduce(mx[:, c:c + 1], bank[4 + c][:, 0:n], AX.X, ALU.max))
                    link(ts(mx[:, 2:4], mx[:, 0:2], -(DH_A ** -0.5), ALU.mult))
                    dve.sem_inc(s_max_ready, 1)

                def soft_mix(i):
                    g = i // 4
                    n = 128 * (g + 1)
                    dve.wait_ge(s_probs_ready, 16 * layer + 2 * i + 2)
                    if 8 * layer + i - 1 > 0:
                        dve.wait_ge(s_att_turned, 8 * layer + i - 1)
                    link(dve.reciprocal(rsum[:, 0:2], sums[:, 0:2]))
                    link(ts(rsum[:, 1:2], rsum[:, 1:2], neglam, ALU.mult))
                    link(ts(amix[:, i % 2, 0:n], probs[:, i % 2, 0, 0:n], rsum[:, 0:1], ALU.mult))
                    stt(amix[:, i % 2, 0:n], probs[:, i % 2, 1, 0:n], rsum[:, 1:2],
                        amix[:, i % 2, 0:n], ALU.mult, ALU.add).then_inc(s_amix_ready, 1)

                rope(0, qkr[:, :, SEQ:TOK], 5, s_qkr_roped)
                for way in range(2):
                    link(tt(qx[:, :, way, :], qkr[:, 0:2, SEQ:TOK], xi[:, :, way, :], ALU.mult))
                dve.sem_inc(s_qx_ready, 1)
                spectrum(0)
                ret_decay(0)
                spectrum(1)
                hyena_out(0)
                rope(1, qk[:, 0:4, SEQ:TOK], 4, s_qa_roped)
                rope(2, qk[:, 4:8, SEQ:TOK], 4, s_qa_roped)
                hyena_out(1)
                yc(0)
                for u in (16, 17):
                    src, free = unit(u)
                    t = 2 * (u - U_GR)
                    dve.wait_ge(s_gr_tanh, 2 * layer + u - 16 + 1)
                    link(stt(gr[:, t:t + 2, :], gr[:, t:t + 2, :], 1.0, src, ALU.add, ALU.mult))
                    dve.sem_inc(free, 1)
                    if u == 16:
                        ret_decay(1)
                yc_gate(0)
                dve.wait_ge(s_ktok_sum, layer + 1)
                for way in range(2):
                    link(tt(kz[:, way, :].rearrange("p (a b) -> p a b", a=4),
                            bank[4][:, 0:256].rearrange("p (a b) -> p a b", a=4),
                            zeta[:, 4 * way:4 * way + 4].unsqueeze(2).broadcast_to([P, 4, 64]),
                            ALU.mult))
                dve.sem_inc(s_bank_free[4], 1)
                dve.sem_inc(s_kz_ready, 1)
                yc(1)
                yc_gate(1)
                for i in range(10):
                    if i < 8:
                        soft_max(i)
                        soft_mix(i)
                    if i - 2 == 3:
                        ya(0)
                ya(1)
                u = U_MERGE
                for half in range(2):
                    for n, branch in enumerate((1, 2, 0)):
                        for dp in range(2):
                            src, free = unit(u)
                            t = 4 * half + 2 * dp
                            gt_ = gates[:, 8 * branch + t:8 * branch + t + 2, :]
                            m = merged[:, t:t + 2, :]
                            tw = tmp[:, :].rearrange("p (a b) -> p a b", a=2)
                            if n == 0:
                                link(stt(m, gt_, 1.0, src, ALU.add, ALU.mult))
                                dve.sem_inc(free, 1)
                            else:
                                link(stt(tw, gt_, 1.0, src, ALU.add, ALU.mult))
                                dve.sem_inc(free, 1)
                                link(tt(m, m, tw, ALU.add))
                            if n == 2:
                                dve.sem_inc(s_merged, 1)
                            u += 1
                for u in range(U_OUT, N_PROJ):
                    src, free = unit(u)
                    for c in range(2):
                        t = 2 * (u - U_OUT) + c
                        for g in range(GROUPS):
                            link(stt(x[:, t, g_cols(g)], src[:, c, g_cols(g)],
                                     modT[:, 16 + t, g:g + 1], x[:, t, g_cols(g)], ALU.mult, ALU.add))
                    dve.sem_inc(free, 1)
                    dve.sem_inc(s_x_mixed, 1)
                dve.sem_inc(s_params_used, 1)
                norm(2 * layer + 1, 1)
                dve.wait_ge(s_logits, layer + 1)
                lg3 = bank[5][:, 0:32].rearrange("p (a b) -> p a b", a=2)

                def per_token(a):
                    return a.unsqueeze(2).broadcast_to([P, 2, N_EXPERTS])

                e_, sel_, tmp_, oh1, oh2 = (rt[:, n, :, :] for n in range(5))
                link(dve.tensor_reduce(red[:, 0:2], lg3, AX.X, ALU.max))
                link(tt(e_, lg3, per_token(red[:, 0:2]), ALU.subtract))
                dve.sem_inc(s_bank_free[5], 1)
                dve.sem_inc(s_logits_shifted, 1)
                dve.wait_ge(s_logits_exp, layer + 1)
                link(dve.tensor_reduce(red[:, 2:4], e_, AX.X, ALU.add))
                link(dve.reciprocal(red[:, 4:6], red[:, 2:4]))
                link(tt(e_, e_, per_token(red[:, 4:6]), ALU.mult))
                link(tt(sel_, e_, H("b_router").unsqueeze(1).broadcast_to([P, 2, 16]), ALU.add))
                s4 = sel_.rearrange("p a (g e) -> p (a g) e", e=EPG)
                link(tt(pair[:, :, 0:3], s4[:, :, 0:3], s4[:, :, 1:4], ALU.add))
                link(tt(pair[:, :, 3:5], s4[:, :, 0:2], s4[:, :, 2:4], ALU.add))
                link(tt(pair[:, :, 5:6], s4[:, :, 0:1], s4[:, :, 3:4], ALU.add))
                link(dve.tensor_reduce(red[:, 8:16], pair[:, :, :], AX.X, ALU.max))
                gs = red[:, 8:16].rearrange("p (a g) -> p a g", a=2)

                def first_max(out, src, n, order):
                    w = order.unsqueeze(1).broadcast_to([P, 2, n])
                    link(dve.tensor_reduce(red[:, 24:26], src, AX.X, ALU.max))
                    link(tt(out, src, red[:, 24:26].unsqueeze(2).broadcast_to([P, 2, n]),
                            ALU.is_equal))
                    link(tt(out, out, w, ALU.mult))
                    link(dve.tensor_reduce(red[:, 26:28], out, AX.X, ALU.max))
                    link(tt(out, out, red[:, 26:28].unsqueeze(2).broadcast_to([P, 2, n]),
                            ALU.is_equal))

                falling = C("xb")
                gm = red[:, 16:24].rearrange("p (a g) -> p a g", a=2)
                first_max(gm, gs, N_GROUPS, falling[:, 0:4])
                link(ts(red[:, 8:16], red[:, 16:24], -1.0, ALU.add, BIG, ALU.mult))
                gm4 = red[:, 16:24].unsqueeze(2).broadcast_to([P, 8, 4])
                gb4 = red[:, 8:16].unsqueeze(2).broadcast_to([P, 8, 4])
                link(tt(s4, s4, gm4, ALU.mult))
                link(tt(s4, s4, gb4, ALU.add))
                first_max(oh1, sel_, N_EXPERTS, falling[:, 0:16])
                link(stt(sel_, oh1, -4.0 * BIG, sel_, ALU.mult, ALU.add))
                first_max(oh2, sel_, N_EXPERTS, falling[:, 0:16])
                tt(oh1, oh1, oh2, ALU.add).then_inc(s_chosen, 1)
                dve.wait_ge(s_chosen, layer + 1)
                for n in (0, 2):
                    dve.wait_ge(s_tokens_turned, 4 * layer + n + 1)
                    b = (4, 6, 7, 4)[n]
                    link(dve.tensor_copy(htok[:, n // 2, 0:512], bank[b][:, :]))
                    dve.sem_inc(s_bank_free[b], 1)
                    dve.sem_inc(s_tokens_copied, 1)
                link(tt(tmp_, oh1, e_, ALU.mult))
                link(dve.tensor_reduce(red[:, 2:4], tmp_, AX.X, ALU.add))
                link(dve.reciprocal(red[:, 4:6], red[:, 2:4]))
                link(tt(tmp_, tmp_, per_token(red[:, 4:6]), ALU.mult))
                gate, rank = rt[:, 5, :, :], rt[:, 4, :, :]
                link(ts(gate, tmp_, 0.5, ALU.mult))
                dve.wait_ge(s_ranked, layer + 1)
                link(tt(rank, bank[5][:, 0:32].rearrange("p (a b) -> p a b", a=2), oh1, ALU.mult))
                count = cnt[:, 2, 0:N_EXPERTS]
                link(dve.tensor_copy(count, bank[5][:, 32:48]))
                dve.sem_inc(s_bank_free[5], 1)
                slots = C("xf")[:, 0:BLOCK]

                def picks(p):
                    n = PAIRS * layer + p
                    if p >= 2:
                        dve.wait_ge(s_gathered, 2 * (n - 1))
                    for g in range(GROUPS):
                        for j in range(2):
                            e, c = 2 * p + j, slice(64 * j, 64 * j + 64)
                            ts(pick[p % 2][:, g, c], slots, rank[:, g, e:e + 1], ALU.is_equal)
                            last = ts(pickg[p % 2][:, g, c], slots, rank[:, g, e:e + 1], ALU.is_equal,
                                      gate[:, g, e:e + 1], ALU.mult)
                    last.then_inc(s_picks, 1)
                    dve.wait_ge(s_picks, n + 1)

                def gathered(p):
                    n = PAIRS * layer + p
                    dve.wait_ge(s_gathered, 2 * n + 1)
                    dve.tensor_copy(flat(hgat[:, 4:8, :]), bank[5][:, :]).then_inc(s_hgat_hi, 1)
                    dve.wait_ge(s_hgat_hi, n + 1)
                    dve.sem_inc(s_bank_free[5], 1)

                def out_high(p):
                    n = PAIRS * layer + p
                    dve.wait_ge(s_y_sum, 2 * n + 2)
                    if n:
                        dve.wait_ge(s_combined, n)
                    dve.tensor_copy(ysb[:, 512:1024], bank[5][:, :]).then_inc(s_y_hi, 1)
                    dve.wait_ge(s_y_hi, n + 1)
                    dve.sem_inc(s_bank_free[5], 1)

                picks(0)
                flags, upto, other = (cnt[:, n, :] for n in range(3))
                for c in (2, 1, 0):
                    link(ts(flags[:, 16 * c:16 * c + 16], count, BLOCK * (c + 1.0), ALU.is_gt))
                src, dst = flags, upto
                step = 1
                while step < OVER * N_EXPERTS:
                    link(dve.tensor_copy(dst[:, 0:step], src[:, 0:step]))
                    link(tt(dst[:, step:], src[:, step:], src[:, :OVER * N_EXPERTS - step], ALU.add))
                    src, dst = dst, (other if dst is upto else upto)
                    step *= 2
                upto = src
                dve.tensor_copy(ints[:, 0:1], upto[:, OVER * N_EXPERTS - 1:]).then_inc(s_more_known, 1)
                gathered(0)
                for p in range(PAIRS):
                    n = PAIRS * layer + p
                    if p + 1 < PAIRS:
                        picks(p + 1)
                    dve.wait_ge(s_ff_tanh, n + 1)
                    if n:
                        dve.wait_ge(s_act_turned, n)
                    link(stt(act, th, 1.0, bank[6][:, :], ALU.add, ALU.mult))
                    dve.sem_inc(s_bank_free[6], 1)
                    tt(act, act, bank[7][:, :], ALU.mult).then_inc(s_act_ready, 1)
                    dve.wait_ge(s_act_ready, n + 1)
                    dve.sem_inc(s_bank_free[7], 1)
                    if p + 1 < PAIRS:
                        gathered(p + 1)
                    if p:
                        out_high(p - 1)
                out_high(PAIRS - 1)

                def more_block(i):
                    n = MORE * layer + i
                    if i:
                        dve.wait_ge(s_more_combined, n)
                    one = tmp[:, 0:48]
                    link(stt(one, upto, i + 1.0, flags, ALU.is_equal, ALU.mult))
                    byexp = tmp[:, 64:80]
                    link(tt(byexp, one[:, 0:16], one[:, 16:32], ALU.add))
                    link(tt(byexp, byexp, one[:, 32:48], ALU.add))
                    link(tt(tmp[:, 96:112], byexp, C("xf")[:, 0:16], ALU.mult))
                    link(dve.tensor_reduce(red[:, 0:1], tmp[:, 96:112], AX.X, ALU.add))
                    link(ts(ints[:, 1:2], red[:, 0:1], -1.0, ALU.add))
                    link(ts(tmp[:, 112:128], one[:, 16:32], 2.0, ALU.mult))
                    link(tt(tmp[:, 112:128], tmp[:, 112:128], one[:, 0:16], ALU.add))
                    link(stt(tmp[:, 112:128], one[:, 32:48], 3.0, tmp[:, 112:128], ALU.mult, ALU.add))
                    link(dve.tensor_reduce(red[:, 1:2], tmp[:, 112:128], AX.X, ALU.add))
                    link(ts(red[:, 1:2], red[:, 1:2], -float(BLOCK), ALU.mult))
                    wide_ = tmp[:, 128:160].rearrange("p (a b) -> p a b", a=2)
                    both = byexp.unsqueeze(1).broadcast_to([P, 2, 16])
                    link(tt(wide_, rank, both, ALU.mult))
                    link(dve.tensor_reduce(red[:, 2:4], wide_, AX.X, ALU.add))
                    link(ts(red[:, 2:4], red[:, 2:4], red[:, 1:2], ALU.add))
                    link(tt(wide_, gate, both, ALU.mult))
                    link(dve.tensor_reduce(red[:, 4:6], wide_, AX.X, ALU.add))
                    link(dve.memset(pick[0], 0.0))
                    link(dve.memset(pickg[0], 0.0))
                    for g in range(GROUPS):
                        link(ts(pick[0][:, g, 0:64], slots, red[:, 2 + g:3 + g], ALU.is_equal))
                        link(ts(pickg[0][:, g, 0:64], slots, red[:, 2 + g:3 + g], ALU.is_equal,
                                red[:, 4 + g:5 + g], ALU.mult))
                    dve.sem_inc(s_more_picked, 1)
                    dve.wait_ge(s_more_gathered, n + 1)
                    link(dve.tensor_copy(scat[0], bank[6][:, 0:TOK]))
                    link(dve.tensor_copy(flat(hgat[:, 0:4, :]), bank[4][:, :]))
                    link(dve.tensor_copy(flat(hgat[:, 4:8, :]), bank[5][:, :]))
                    dve.sem_inc(s_more_hgat, 1)
                    dve.wait_ge(s_more_tanh, n + 1)
                    link(stt(act, th, 1.0, bank[6][:, :], ALU.add, ALU.mult))
                    link(tt(act, act, bank[7][:, :], ALU.mult))
                    dve.sem_inc(s_more_act, 1)
                    dve.wait_ge(s_more_turned, n + 1)
                    link(dve.tensor_copy(flat(actT[0]), bank[4][:, :]))
                    dve.sem_inc(s_more_actT, 1)
                    dve.wait_ge(s_more_ysum, n + 1)
                    link(dve.tensor_copy(ysb[:, 0:512], bank[6][:, :]))
                    link(dve.tensor_copy(ysb[:, 512:1024], bank[7][:, :]))
                    dve.sem_inc(s_more_y, 1)

                blocks = dve.value_load(ints[0:1, 0:1], min_val=0, max_val=MORE)
                dve.wait_ge(s_combined, PAIRS * (layer + 1))
                for i in range(MORE):
                    before = links[0]
                    with dve.If(blocks > i):
                        more_block(i)
                    with dve.Else():
                        for event in (s_more_picked, s_more_hgat, s_more_act, s_more_actT, s_more_y):
                            dve.sem_inc(event, 1)
                        dve.sem_inc(s_vector_link, links[0] - before)
                dve.wait_ge(s_experts_done, layer + 1)
                for b in range(4, 8):
                    dve.sem_inc(s_bank_free[b], 1)
                for b in range(4):
                    src = tiles(b)
                    for c in range(2):
                        t = 2 * b + c
                        for g in range(GROUPS):
                            link(stt(x[:, t, g_cols(g)], src[:, c, g_cols(g)],
                                     modT[:, 40 + t, g:g + 1], x[:, t, g_cols(g)], ALU.mult, ALU.add))
                    dve.sem_inc(s_bank_free[b], 1)
                    dve.sem_inc(s_x_moe, 1)
            norm(2 * DEPTH, None)
            dve.sem_inc(s_y_ready, 1)


def lay_out(a):
    def blocks(w, c0, width):
        k = w.shape[0] // P
        return w[:, c0:c0 + width].reshape(k, P, width).transpose(1, 0, 2).reshape(P, k * width)

    pieces = []
    for l in range(DEPTH):
        pieces += [blocks(a["w_ada"][l], c, 256) for c in range(0, 6 * D, 256)]
        pieces += [blocks(a["w_in"][l], c, 256) for c in W_IN_ORDER]
        pieces += [blocks(a["w_gate"][l], c, 256) for c in range(0, 3 * D, 256)]
        for half in range(2):
            pieces += [blocks(a[n][l], 512 * half, 512) for n in ("w_branch_b", "w_branch_c", "w_branch_a")]
        pieces += [blocks(a["w_out"][l], c, 256) for c in range(0, D, 256)]

    weights = np.stack(pieces).reshape(DEPTH, DENSE_PIECES, P, PIECE)
    experts = np.stack([np.stack([
        np.stack([blocks(a["moe_w1"][l, e], 0, 256), blocks(a["moe_w3"][l, e], 0, 256),
                  blocks(a["moe_w1"][l, e], 256, 256), blocks(a["moe_w3"][l, e], 256, 256),
                  blocks(a["moe_w2"][l, e], 0, 512), blocks(a["moe_w2"][l, e], 512, 512)])
        for e in range(N_EXPERTS)]) for l in range(DEPTH)])

    def rows(v):
        return v.reshape(-1, P).T

    params = np.zeros((DEPTH, P, N_PAR), np.float32)
    for l in range(DEPTH):
        def put(name, v):
            params[l, :v.shape[0], PAR[name][0]:PAR[name][1]] = v

        put("b_ada", rows(a["b_ada"][l]))
        put("norm1", rows(a["norm1_g"][l]))
        put("norm2", rows(a["norm2_g"][l]))
        put("conv_w", rows(a["hy_conv_w"][l]))
        put("conv_b", rows(a["hy_conv_b"][l]))
        put("skip", rows(a["hy_skip"][l]))
        put("b_gate", rows(a["b_gate"][l]))
        put("subln", rows(a["attn_subln_g"][l]))
        put("lam", np.broadcast_to(a["attn_lambda"][l].reshape(1, -1), (P, 4 * DH_A)))
        r = a["ret_decay_exp"][l]
        put("rde", np.broadcast_to(r.reshape(1, -1), (P, 2 * H_C)))
        put("rde_q", np.repeat(r.reshape(2, 2, 2).transpose(2, 1, 0).reshape(2, 4), 64, axis=0))
        put("f_w1", a["hy_f_w1"][l])
        put("f_b1", a["hy_f_b1"][l].reshape(-1, 1))
        put("f_w2", a["hy_f_w2"][l])
        put("f_b2", a["hy_f_b2"][l].reshape(-1, 1))
        put("f_w3", a["hy_f_w3"][l])
    shared = np.zeros((P, N_SHD), np.float32)
    shared[:, SHD["final"][0]:SHD["final"][1]] = rows(a["final_g"])
    shared[:, SHD["router"][0]:SHD["router"][1]] = blocks(a["w_router"], 0, N_EXPERTS)
    shared[:, SHD["b_router"][0]:SHD["b_router"][1]] = np.broadcast_to(a["b_router"].reshape(1, -1), (P, 16))
    shared[:, SHD["cond"][0]:SHD["cond"][1]] = np.stack([rows(a["c_ctx"]), rows(a["c"][0])], -1).reshape(P, 16)
    x = np.concatenate([a["x_prompt"][0], a["x_sample"][0]], 0)
    x_in = x.T.reshape(KT, P, TOK).transpose(1, 0, 2)
    k_cache = a["cache_attn_k"][0].transpose(0, 3, 2, 1)
    v_cache = a["cache_attn_v"][0].reshape(DEPTH, SEQ, H_A * DV_A)
    s = a["state_retention"][0]
    s_cache = np.zeros((DEPTH, P, H_C, 2, DV_C), np.float32)
    for hh in range(H_C):
        r = 64 * (hh % 2)
        s_cache[:, r:r + 64, hh] = s[:, :, hh].transpose(0, 2, 1, 3)
    out = dict(weights=weights, experts=experts, params=params, consts=constant_columns(), shared=shared, x_in=x_in,
               k_cache=k_cache, v_cache=v_cache, s_cache=s_cache)
    return {n: np.ascontiguousarray(v) for n, v in out.items()}


_OUTS = [("y_out", (P, KT, TOK)), ("k_out", (DEPTH, P, H_A, SEQ)), ("v_out", (DEPTH, SEQ, H_A * DV_A)),
         ("s_out", (DEPTH, 2, DK_C, H_C * DV_C))]


def kernel(**inputs):
    import concourse.bacc as _bacc
    from concourse.bass_utils import run_bass_kernel_spmd as _run

    nc = _bacc.Bacc("TRN2", target_bir_lowering=False, num_devices=1)
    data = lay_out({n: np.asarray(v) for n, v in inputs.items()})
    arrays, args = {}, []
    for name, a in data.items():
        arrays[f"in_{name}"] = a
        args.append(nc.dram_tensor(f"in_{name}", a.shape, F32, kind="ExternalInput").ap())
    for name, shape in _OUTS:
        args.append(nc.dram_tensor(name, shape, F32, kind="ExternalOutput").ap())
    trunk_program(nc, *args)
    r = _run(nc, [arrays], core_ids=[0]).results[0]
    y = r["y_out"].transpose(2, 1, 0).reshape(GROUPS, 1, SEQ, D)
    new_k = r["k_out"].transpose(0, 3, 2, 1)[None]
    new_v = r["v_out"].reshape(1, DEPTH, SEQ, H_A, DV_A)
    new_s = r["s_out"].reshape(DEPTH, 2, DK_C, H_C, DV_C).transpose(0, 1, 3, 2, 4)[None]
    return y[0], y[1], new_k, new_v, new_s
```
